# Optimizing a Trainium2 kernel written in Bass

```python
import math
import jax
import jax.numpy as jnp
from jax import lax
import numpy as np

D_MODEL = 1024
BATCH = 1
SEQ = 256
DEPTH = 1
DEC_BATCH = 8
DEC_SEQ = 4
PAST_LEN = 1024
PAGE_SIZE = 128

NSA_HEADS = 8
NSA_KV_HEADS = 2
NSA_HEAD_DIM = 64
NSA_GROUP = NSA_HEADS // NSA_KV_HEADS
CMP_STRIDE = 16
CMP_BLOCK = 2 * CMP_STRIDE
CMP_HIDDEN = 256
SLC_BLOCK = 64
SLC_TOPK = 16
WINDOW = 512
NSA_QBLOCK = 64
SEL_FORCED = 1.0e4
ROPE_THETA = 10000.0
NSA_Q_W = NSA_HEADS * NSA_HEAD_DIM
NSA_KV_W = NSA_KV_HEADS * NSA_HEAD_DIM
HG_HEADS = 4
HG_DK = 128
HG_DV = 128
HG_CHUNK = 64
HG_W = HG_HEADS * HG_DK
HG_VW = HG_HEADS * HG_DV
N_EXPERTS = 32
TOP_K = 4
D_FF = D_MODEL
SWIGLU_LIMIT = 7.0
SWIGLU_ALPHA = 1.702
MOE_BLOCK = 256
LN_EPS = 1e-5
RMS_EPS = 1e-6
DN_ALPHA = (2 * DEPTH) ** 0.25
DN_BETA = (8 * DEPTH) ** -0.25
SPLITS = (NSA_Q_W, 6 * NSA_KV_W, 3 * NSA_HEADS, HG_W, HG_W, HG_VW, HG_VW, D_MODEL, D_MODEL)
D_IN = sum(SPLITS)

kernel_name = "nsa_hgrn2_gated_merge_moe_decoder_step"

def _layernorm(x, g, b):
    xf = x.astype(jnp.float32)
    mu = jnp.mean(xf, axis=-1, keepdims=True)
    var = jnp.mean(jnp.square(xf - mu), axis=-1, keepdims=True)
    return ((xf - mu) * lax.rsqrt(var + LN_EPS) * g + b).astype(x.dtype)

def _rope(x, pos):
    half = x.shape[-1] // 2
    inv = ROPE_THETA ** (-jnp.arange(half, dtype=jnp.float32) / half)
    ang = pos.astype(jnp.float32)[:, None] * inv[None, :]
    cos = jnp.cos(ang)[None, :, None, :]
    sin = jnp.sin(ang)[None, :, None, :]
    x1 = x[..., :half].astype(jnp.float32)
    x2 = x[..., half:].astype(jnp.float32)
    return jnp.concatenate([x1 * cos - x2 * sin, x2 * cos + x1 * sin], axis=-1).astype(x.dtype)

def _masked_softmax(s, mask, axis):
    s = jnp.where(mask, s.astype(jnp.float32), -jnp.inf)
    m = jnp.max(s, axis=axis, keepdims=True)
    m = jnp.where(jnp.isfinite(m), m, 0.0)
    e = jnp.exp(s - m)
    d = jnp.sum(e, axis=axis, keepdims=True)
    return e / jnp.where(d > 0, d, 1.0)

def _compress(rows, pe, w1, w2):
    B, T, G, Dh = rows.shape
    nfull = T // CMP_STRIDE
    ch = rows[:, :nfull * CMP_STRIDE].reshape(B, nfull, CMP_STRIDE, G, Dh)
    blk = jnp.concatenate([ch[:, :-1], ch[:, 1:]], axis=2) + pe[None, None, :, None, :]
    flat = blk.transpose(0, 1, 3, 2, 4).reshape(B, nfull - 1, G, CMP_BLOCK * Dh)
    return jax.nn.gelu(flat @ w1) @ w2

def _compress_kv(cmp_rows, cmp_params):
    pe_ck, w_ck1, w_ck2, pe_cv, w_cv1, w_cv2 = cmp_params
    ck = _compress(cmp_rows[:, :, 0], pe_ck, w_ck1, w_ck2)
    cv = _compress(cmp_rows[:, :, 1], pe_cv, w_cv1, w_cv2)
    return ck, cv

def _nsa_attend(q, qpos, ck, cv, gather_sel, nsb, wkv, wpos, gates):
    B, Tq = q.shape[:2]
    G, Hg, Dh = NSA_KV_HEADS, NSA_GROUP, NSA_HEAD_DIM
    scale = Dh ** -0.5
    qn = q.reshape(B, Tq, G, Hg, Dh)
    qr = _rope(q, qpos).reshape(B, Tq, G, Hg, Dh)
    nc = ck.shape[1]
    cidx = jnp.arange(nc, dtype=jnp.int32)
    cmask = (cidx[None, :] * CMP_STRIDE + CMP_BLOCK - 1 <= qpos[:, None])[None, :, None, None, :]
    pc = _masked_softmax(jnp.einsum('btghd,bcgd->btghc', qn, ck) * scale, cmask, -1)
    o_cmp = jnp.einsum('btghc,bcgd->btghd', pc, cv.astype(jnp.float32))
    sidx = jnp.arange(nsb, dtype=jnp.int32)
    cover = ((cidx[:, None] * CMP_STRIDE < (sidx[None, :] + 1) * SLC_BLOCK)
             & (cidx[:, None] * CMP_STRIDE + CMP_BLOCK > sidx[None, :] * SLC_BLOCK)).astype(jnp.float32)
    imp = jnp.einsum('btgc,cs->btgs', jnp.sum(pc, axis=3), cover)
    cur = (qpos // SLC_BLOCK)[:, None]
    valid = (sidx[None, :] * SLC_BLOCK <= qpos[:, None])[None, :, None, :]
    forced = ((sidx[None, :] == 0) | (sidx[None, :] == cur) | (sidx[None, :] == cur - 1))[None, :, None, :]
    score = jnp.where(forced, SEL_FORCED, jnp.where(valid, imp, -jnp.inf))
    _, sel = lax.top_k(score, min(SLC_TOPK, nsb))
    sel = sel.transpose(0, 2, 1, 3)
    kv_sel = gather_sel(sel)
    kpos = sel[..., None] * SLC_BLOCK + jnp.arange(SLC_BLOCK, dtype=jnp.int32)
    smask = (kpos <= qpos[None, None, :, None, None])[:, :, :, None]
    ps = _masked_softmax(jnp.einsum('btghd,bgtsld->bgthsl', qr, kv_sel[..., 0, :]) * scale, smask, (-2, -1))
    o_slc = jnp.einsum('bgthsl,bgtsld->btghd', ps, kv_sel[..., 1, :].astype(jnp.float32))
    dpos = qpos[:, None] - wpos[None, :]
    wmask = ((dpos >= 0) & (dpos < WINDOW) & (wpos[None, :] >= 0))[None, :, None, None, :]
    pw = _masked_softmax(jnp.einsum('btghd,blgd->btghl', qr, wkv[:, :, 0]) * scale, wmask, -1)
    o_win = jnp.einsum('btghl,blgd->btghd', pw, wkv[:, :, 1].astype(jnp.float32))
    g = jax.nn.sigmoid(gates.astype(jnp.float32)).reshape(B, Tq, 3, G, Hg, 1)
    o = g[:, :, 0] * o_cmp + g[:, :, 1] * o_slc + g[:, :, 2] * o_win
    return o.reshape(B, Tq, NSA_Q_W).astype(q.dtype)

def _nsa_rows(kv6, pos):
    cmp_rows = kv6[:, :, 0:2]
    slc_rows = jnp.stack([_rope(kv6[:, :, 2], pos), kv6[:, :, 3]], axis=2)
    win_rows = jnp.stack([_rope(kv6[:, :, 4], pos), kv6[:, :, 5]], axis=2)
    return cmp_rows, slc_rows, win_rows

def _nsa_prompt(q, kv6, gates, cmp_params):
    B, T = q.shape[:2]
    G, Dh = NSA_KV_HEADS, NSA_HEAD_DIM
    pos = jnp.arange(T, dtype=jnp.int32)
    cmp_rows, slc_rows, win_rows = _nsa_rows(kv6, pos)
    ck, cv = _compress_kv(cmp_rows, cmp_params)
    nsb = T // SLC_BLOCK
    slc_blocks = slc_rows.reshape(B, nsb, SLC_BLOCK, 2, G, Dh)
    bi = jnp.arange(B)[:, None, None, None]
    gi = jnp.arange(G)[None, :, None, None]

    def gather_sel(sel):
        return slc_blocks[bi, sel, :, :, gi, :]

    win_pad = jnp.pad(win_rows, ((0, 0), (WINDOW, 0), (0, 0), (0, 0), (0, 0)))
    qb = math.gcd(T, NSA_QBLOCK)
    nb = T // qb
    q_blocks = q.reshape(B, nb, qb, NSA_HEADS, Dh).transpose(1, 0, 2, 3, 4)
    g_blocks = gates.reshape(B, nb, qb, 3 * NSA_HEADS).transpose(1, 0, 2, 3)

    def body(args):
        i, qi, gblk = args
        start = i * qb
        qpos = start + jnp.arange(qb, dtype=jnp.int32)
        wkv = lax.dynamic_slice_in_dim(win_pad, start, WINDOW + qb, axis=1)
        wpos = start - WINDOW + jnp.arange(WINDOW + qb, dtype=jnp.int32)
        return _nsa_attend(qi, qpos, ck, cv, gather_sel, nsb, wkv, wpos, gblk)

    out = lax.map(body, (jnp.arange(nb, dtype=jnp.int32), q_blocks, g_blocks))
    out = out.transpose(1, 0, 2, 3).reshape(B, T, NSA_Q_W)
    keep = min(WINDOW, T)
    return out, cmp_rows, slc_rows, win_rows[:, T - keep:]

def _nsa_sample(q, kv6, gates, cmp_params, cache_cmp_kv, cache_slc_kv, win_buf, page_table, layer):
    B, T = q.shape[:2]
    G, Dh = NSA_KV_HEADS, NSA_HEAD_DIM
    page = cache_cmp_kv.shape[2]
    past = page_table.shape[1] * page
    pos = past + jnp.arange(T, dtype=jnp.int32)
    cmp_rows, slc_rows, win_rows = _nsa_rows(kv6, pos)
    past_cmp = cache_cmp_kv[layer, page_table].reshape(B, past, 2, G, Dh)
    ck, cv = _compress_kv(jnp.concatenate([past_cmp, cmp_rows], axis=1), cmp_params)
    nsb = -(-(past + T) // SLC_BLOCK)
    npb = past // SLC_BLOCK
    n_new = nsb - npb
    r = page // SLC_BLOCK
    new_blocks = jnp.pad(slc_rows, ((0, 0), (0, n_new * SLC_BLOCK - T), (0, 0), (0, 0), (0, 0)))
    new_blocks = new_blocks.reshape(B, n_new, SLC_BLOCK, 2, G, Dh)
    pool_blocks = cache_slc_kv.reshape(cache_slc_kv.shape[0], -1, SLC_BLOCK, 2, G, Dh)
    bi = jnp.arange(B)[:, None, None, None]
    gi = jnp.arange(G)[None, :, None, None]

    def gather_sel(sel):
        jp = jnp.minimum(sel, npb - 1)
        phys = page_table[bi, jp // r] * r + jp % r
        from_pool = pool_blocks[layer, phys, :, :, gi, :]
        from_new = new_blocks[bi, jnp.clip(sel - npb, 0, n_new - 1), :, :, gi, :]
        return jnp.where((sel >= npb)[..., None, None, None], from_new, from_pool)

    wb = win_buf.shape[1]
    wkv = jnp.concatenate([win_buf, win_rows], axis=1)
    wpos = past - wb + jnp.arange(wb + T, dtype=jnp.int32)
    out = _nsa_attend(q, pos, ck, cv, gather_sel, nsb, wkv, wpos, gates)
    return out, cmp_rows, slc_rows, wkv[:, T:]

def _hgrn2(hq, hf, hi, hg, lb, norm_w, s0):
    B, T, H, Dk = hq.shape
    Dv = hi.shape[-1]
    q = jax.nn.silu(hq.astype(jnp.float32))
    f = lb + (1.0 - lb) * jax.nn.sigmoid(hf.astype(jnp.float32))
    logf = jnp.log(f)
    k = 1.0 - f
    iv = hi.astype(jnp.float32)
    c = math.gcd(T, HG_CHUNK)
    n = T // c

    def to_chunks(a):
        return a.reshape(B, n, c, H, a.shape[-1]).transpose(1, 0, 3, 2, 4)

    causal = jnp.tril(jnp.ones((c, c), dtype=bool))[:, :, None]

    def step(S, xs):
        qc, kc, lc, ic = xs
        b = jnp.cumsum(lc, axis=2)
        diff = b[:, :, :, None, :] - b[:, :, None, :, :]
        dec = jnp.exp(jnp.where(causal, diff, -jnp.inf))
        att = jnp.einsum('bhtk,bhsk,bhtsk->bhts', qc, kc, dec)
        o = att @ ic + jnp.einsum('bhtk,bhkv->bhtv', qc * jnp.exp(b), S)
        bl = b[:, :, -1, :]
        S = jnp.exp(bl)[..., None] * S + jnp.einsum('bhsk,bhsv->bhkv', kc * jnp.exp(bl[:, :, None, :] - b), ic)
        return S, o

    S, o = lax.scan(step, s0.astype(jnp.float32), (to_chunks(q), to_chunks(k), to_chunks(logf), to_chunks(iv)))
    o = o.transpose(1, 0, 3, 2, 4).reshape(B, T, H, Dv)
    o = o * lax.rsqrt(jnp.mean(jnp.square(o), axis=-1, keepdims=True) + RMS_EPS) * norm_w
    o = o * jax.nn.silu(hg.astype(jnp.float32))
    return o.reshape(B, T, H * Dv).astype(hq.dtype), S.astype(s0.dtype)

def _moe(x, w_router, b_router, w_gu, b_gu, w_dn, b_dn):
    shp = x.shape
    xt = x.reshape(-1, shp[-1])
    N = xt.shape[0]
    logits = (xt @ w_router + b_router).astype(jnp.float32)
    top_v, top_e = lax.top_k(logits, TOP_K)
    gate = jax.nn.softmax(top_v, axis=-1)
    A = N * TOP_K
    e_flat = top_e.reshape(-1)
    tok_flat = jnp.arange(A, dtype=jnp.int32) // TOP_K
    order = jnp.argsort(e_flat)
    e_s, tok_s, w_s = e_flat[order], tok_flat[order], gate.reshape(-1)[order]
    blk = max(8, min(MOE_BLOCK, A // N_EXPERTS))
    nblk = A // blk + N_EXPERTS
    counts = jnp.bincount(e_flat, length=N_EXPERTS)
    pcounts = (counts + blk - 1) // blk * blk
    pend = jnp.cumsum(pcounts)
    pstart = pend - pcounts
    start = jnp.cumsum(counts) - counts
    dest = pstart[e_s] + jnp.arange(A, dtype=jnp.int32) - start[e_s]
    xs = jnp.zeros((nblk * blk, shp[-1]), x.dtype).at[dest].set(xt[tok_s])
    bexp = jnp.minimum(jnp.sum(jnp.arange(nblk)[:, None] * blk >= pend[None, :], axis=1), N_EXPERTS - 1)

    def expert_block(args):
        xb, e = args
        h = xb @ w_gu[e] + b_gu[e]
        gt = jnp.minimum(h[:, :D_FF], SWIGLU_LIMIT)
        up = jnp.clip(h[:, D_FF:], -SWIGLU_LIMIT, SWIGLU_LIMIT)
        return ((up + 1.0) * (gt * jax.nn.sigmoid(SWIGLU_ALPHA * gt))) @ w_dn[e] + b_dn[e]

    ys = lax.map(expert_block, (xs.reshape(nblk, blk, shp[-1]), bexp)).reshape(nblk * blk, shp[-1])
    y = jnp.zeros((N, shp[-1]), jnp.float32).at[tok_s].add(w_s[:, None] * ys[dest].astype(jnp.float32))
    return y.astype(x.dtype).reshape(shp)

def _project_in(x, w_in):
    B, T, _ = x.shape
    points = [int(v) for v in np.cumsum(SPLITS)[:-1]]
    q, kv, ng, hq, hf, hi, hg, ga, gb = jnp.split(x @ w_in, points, axis=-1)
    return (q.reshape(B, T, NSA_HEADS, NSA_HEAD_DIM),
            kv.reshape(B, T, 6, NSA_KV_HEADS, NSA_HEAD_DIM), ng,
            hq.reshape(B, T, HG_HEADS, HG_DK), hf.reshape(B, T, HG_HEADS, HG_DK),
            hi.reshape(B, T, HG_HEADS, HG_DV), hg.reshape(B, T, HG_HEADS, HG_DV), ga, gb)

def _finish(x, nsa_o, hg_o, ga, gb, w_pa, w_pb, w_o, ln1_g, ln1_b, moe_w, ln2_g, ln2_b):
    mix = (jax.nn.sigmoid(ga) * (nsa_o @ w_pa) + jax.nn.sigmoid(gb) * (hg_o @ w_pb)) @ w_o
    h = _layernorm(DN_ALPHA * x + mix, ln1_g, ln1_b)
    return _layernorm(DN_ALPHA * h + _moe(h, *moe_w), ln2_g, ln2_b)

def setup_inputs(seed: int = 0) -> dict:
    key = jax.random.key(seed)
    ks = jax.random.split(key, 40)
    f32 = jnp.float32
    n_pages = PAST_LEN // PAGE_SIZE
    n_used = DEC_BATCH * n_pages
    n_pool = (5 * n_used + 3) // 4
    wbuf = min(WINDOW, PAST_LEN)
    G, Dh = NSA_KV_HEADS, NSA_HEAD_DIM

    def nrm(k, shape, scale):
        return jax.random.normal(k, shape, f32) * scale

    return {
        "x_prompt": nrm(ks[0], (BATCH, SEQ, D_MODEL), 1.0),
        "x_sample": nrm(ks[1], (DEC_BATCH, DEC_SEQ, D_MODEL), 1.0),
        "cache_cmp_kv": nrm(ks[2], (DEPTH, n_pool, PAGE_SIZE, 2, G, Dh), 1.0),
        "cache_slc_kv": nrm(ks[3], (DEPTH, n_pool, PAGE_SIZE, 2, G, Dh), 1.0),
        "cache_win_kv": nrm(ks[4], (DEPTH, DEC_BATCH, wbuf, 2, G, Dh), 1.0),
        "state_hgrn": nrm(ks[5], (DEPTH, DEC_BATCH, HG_HEADS, HG_DK, HG_DV), 1.0),
        "page_table": jax.random.permutation(ks[6], n_pool)[:n_used].reshape(DEC_BATCH, n_pages).astype(jnp.int32),
        "w_in": nrm(ks[7], (DEPTH, D_MODEL, D_IN), D_MODEL ** -0.5),
        "pe_ck": nrm(ks[8], (DEPTH, CMP_BLOCK, Dh), 0.5),
        "w_ck1": nrm(ks[9], (DEPTH, CMP_BLOCK * Dh, CMP_HIDDEN), (CMP_BLOCK * Dh) ** -0.5),
        "w_ck2": nrm(ks[10], (DEPTH, CMP_HIDDEN, Dh), CMP_HIDDEN ** -0.5),
        "pe_cv": nrm(ks[11], (DEPTH, CMP_BLOCK, Dh), 0.5),
        "w_cv1": nrm(ks[12], (DEPTH, CMP_BLOCK * Dh, CMP_HIDDEN), (CMP_BLOCK * Dh) ** -0.5),
        "w_cv2": nrm(ks[13], (DEPTH, CMP_HIDDEN, Dh), CMP_HIDDEN ** -0.5),
        "hg_lb_logits": nrm(ks[14], (DEPTH + 1, HG_W), 0.5),
        "hg_norm_w": 1.0 + nrm(ks[15], (DEPTH, HG_DV), 0.02),
        "w_pa": nrm(ks[16], (DEPTH, NSA_Q_W, D_MODEL), NSA_Q_W ** -0.5),
        "w_pb": nrm(ks[17], (DEPTH, HG_VW, D_MODEL), HG_VW ** -0.5),
        "w_o": nrm(ks[18], (DEPTH, D_MODEL, D_MODEL), DN_BETA * D_MODEL ** -0.5),
        "ln1_g": 1.0 + nrm(ks[19], (DEPTH, D_MODEL), 0.02),
        "ln1_b": nrm(ks[20], (DEPTH, D_MODEL), 0.02),
        "w_router": nrm(ks[21], (DEPTH, D_MODEL, N_EXPERTS), D_MODEL ** -0.5),
        "b_router": nrm(ks[22], (DEPTH, N_EXPERTS), 0.01),
        "w_gu": nrm(ks[23], (DEPTH, N_EXPERTS, D_MODEL, 2 * D_FF), D_MODEL ** -0.5),
        "b_gu": nrm(ks[24], (DEPTH, N_EXPERTS, 2 * D_FF), 0.01),
        "w_dn": nrm(ks[25], (DEPTH, N_EXPERTS, D_FF, D_MODEL), DN_BETA * D_FF ** -0.5),
        "b_dn": nrm(ks[26], (DEPTH, N_EXPERTS, D_MODEL), 0.01),
        "ln2_g": 1.0 + nrm(ks[27], (DEPTH, D_MODEL), 0.02),
        "ln2_b": nrm(ks[28], (DEPTH, D_MODEL), 0.02),
    }

def reference(x_prompt, x_sample, cache_cmp_kv, cache_slc_kv, cache_win_kv, state_hgrn, page_table,
              w_in, pe_ck, w_ck1, w_ck2, pe_cv, w_cv1, w_cv2, hg_lb_logits, hg_norm_w,
              w_pa, w_pb, w_o, ln1_g, ln1_b, w_router, b_router, w_gu, b_gu, w_dn, b_dn, ln2_g, ln2_b):
    lb_all = jnp.cumsum(jax.nn.softmax(hg_lb_logits.astype(jnp.float32), axis=0), axis=0)
    hp, hs = x_prompt, x_sample
    cmp_p, cmp_s, slc_p, slc_s, win_p, win_s, hg_p, hg_s = [], [], [], [], [], [], [], []
    for l in range(DEPTH):
        cmp_params = (pe_ck[l], w_ck1[l], w_ck2[l], pe_cv[l], w_cv1[l], w_cv2[l])
        lb = lb_all[l].reshape(HG_HEADS, HG_DK)
        moe_w = (w_router[l], b_router[l], w_gu[l], b_gu[l], w_dn[l], b_dn[l])
        q, kv6, ng, hq, hf, hi, hg, ga, gb = _project_in(hp, w_in[l])
        nsa_o, c_rows, s_rows, w_rows = _nsa_prompt(q, kv6, ng, cmp_params)
        s0 = jnp.zeros((hp.shape[0], HG_HEADS, HG_DK, HG_DV), hp.dtype)
        hg_o, s_new = _hgrn2(hq, hf, hi, hg, lb, hg_norm_w[l], s0)
        hp = _finish(hp, nsa_o, hg_o, ga, gb, w_pa[l], w_pb[l], w_o[l], ln1_g[l], ln1_b[l], moe_w, ln2_g[l], ln2_b[l])
        cmp_p.append(c_rows)
        slc_p.append(s_rows)
        win_p.append(w_rows)
        hg_p.append(s_new)
        q, kv6, ng, hq, hf, hi, hg, ga, gb = _project_in(hs, w_in[l])
        nsa_o, c_rows, s_rows, w_state = _nsa_sample(q, kv6, ng, cmp_params, cache_cmp_kv, cache_slc_kv,
                                                     cache_win_kv[l], page_table, l)
        hg_o, s_new = _hgrn2(hq, hf, hi, hg, lb, hg_norm_w[l], state_hgrn[l])
        hs = _finish(hs, nsa_o, hg_o, ga, gb, w_pa[l], w_pb[l], w_o[l], ln1_g[l], ln1_b[l], moe_w, ln2_g[l], ln2_b[l])
        cmp_s.append(c_rows)
        slc_s.append(s_rows)
        win_s.append(w_state)
        hg_s.append(s_new)
    return (hp, hs, jnp.stack(cmp_p), jnp.stack(cmp_s), jnp.stack(slc_p), jnp.stack(slc_s),
            jnp.stack(win_p), jnp.stack(win_s), jnp.stack(hg_p), jnp.stack(hg_s))


_drawn_inputs = setup_inputs


def setup_inputs(seed=0):
    import zlib

    import numpy as np

    out = dict(_drawn_inputs(seed))
    spreads = {}
    factors = {'cache_cmp_kv': 2.919,
     'cache_slc_kv': 7.103,
     'pe_ck': 4.032,
     'hg_norm_w': 4.34,
     'b_router': 3.491,
     'b_gu': 8.0,
     'b_dn': 8.0,
     'ln2_g': 3.094,
     'ln2_b': 2.739}
    for name, (base, spread) in spreads.items():
        noise = np.random.default_rng([zlib.crc32(name.encode()), seed]).standard_normal(out[name].shape)
        drawn = base * np.exp(spread * noise) if base else spread * noise
        out[name] = jnp.asarray(drawn.astype(out[name].dtype))
    for name, factor in factors.items():
        out[name] = (out[name] * factor).astype(out[name].dtype)
    return out
```

```python
import math
from contextlib import ExitStack

import numpy as np

import concourse.bass as bass
from concourse import mybir

F32 = mybir.dt.float32
I32 = mybir.dt.int32
ALU = mybir.AluOpType
ACT = mybir.ActivationFunctionType
AXX = mybir.AxisListType.X

P = 128
D = 1024
KD = D // P
SEQ, DB, DT = 256, 8, 4
NS = DB * DT
NT = SEQ + NS
TILES = [(0, P), (P, P), (SEQ, NS)]
PAST, PAGE, NPOOL = 1024, 128, 80
NPG = PAST // PAGE
G, HG, DH = 2, 4, 64
GD = G * DH
WIN = 512
DEPTH = 1
NCS, NCP = PAST // 16 - 1, SEQ // 16 - 1
HID = 256
LP = 16
SLC = 64
NSB = PAST // SLC
HH, DK = 4, 128
CH = 64
NE = 32
CAP = 64
DF = D
SCALE = DH ** -0.5
NEG = -1.0e30
ALPHA = (2 * DEPTH) ** 0.25
D_IN = 5400
C_Q, C_KV, C_HQ, C_HF, C_HI, C_HG, C_GA, C_GB = 0, 512, 1304, 1816, 2328, 2840, 3352, 4376
KVW = 6 * GD + 3 * G * HG

RMS_EPS, LN_EPS = 1e-6, 1e-5
ITS = [(g, qt) for g in range(G) for qt in range(2)]
PREV_ACT = [sum(4 * qt for _, qt in ITS[:n]) for n in range(len(ITS))]
LEVELS = [0, 1, 2, 4, 8, 16, 32]
LEVEL_TILES = [3 if lv < DT else 2 for lv in LEVELS]


def level_tiles_before(n, first=0):
    return sum(LEVEL_TILES[first:n])

def constant_parts():
    i = np.arange(P)
    parts = {}
    parts["ident"] = np.eye(P)
    parts["before"] = (i[:, None] < i[None, :])
    parts["ones"] = np.ones((P, P))
    parts["same_group"] = (i[:, None] // HG == i[None, :] // HG)
    parts["causal"] = np.where(i[None, :] <= i[:, None], 0.0, NEG)
    c = np.arange(NCP)
    qp = np.arange(SEQ).reshape(2, P)
    cm = np.where(c[None, None, :] * 16 + 31 <= qp[:, :, None], 0.0, NEG)
    parts["cmp_mask"] = cm.transpose(1, 0, 2).reshape(P, 2 * NCP)
    parts["cmp_any"] = (qp >= 31).T
    r = np.arange(P)
    new = []
    for s in range(2):
        tok, b = s * 16 + r // 8, (s * 16 + r // 8) // DT
        k = np.arange(NS)
        new.append(np.where((k[None, :] // DT == b[:, None]) & (k[None, :] <= tok[:, None]), 0.0, NEG))
    parts["new_mask"] = np.concatenate(new, 1)
    parts["win_mask"] = np.where(np.arange(DT)[None, :] >= 1 + (r // 8 % DT)[:, None], 0.0, NEG)
    for lv in LEVELS[1:]:
        blk = i // (2 * lv)
        parts[f"level{lv}"] = ((blk[:, None] == blk[None, :]) & (i[:, None] % (2 * lv) < lv)
                               & (i[None, :] % (2 * lv) >= lv))
    t = np.arange(NT)
    starts = np.where(t < SEQ, t % CH == 0, (t - SEQ) % DT == 0)
    parts["carry"] = np.where(starts, 0.0, 1.0)[None, :].repeat(P, 0)
    parts["own_batch"] = (i[:, None] % NS // DT == np.arange(DB)[None, :])
    parts["slot_of"] = np.arange(CAP)[None, :].repeat(P, 0)
    parts["block_no"] = np.arange(1, 15)[None, :].repeat(P, 0)
    parts["valid"] = np.arange(3 * P).reshape(3, P).T < NT
    parts["caps"] = (CAP * np.arange(1, 5))[None, :].repeat(P, 0)
    half = DH // 2
    inv = (10000.0 ** (-np.arange(half) / half)).astype(np.float32)
    pos = np.concatenate([np.arange(SEQ), PAST + np.tile(np.arange(DT), DB)]).astype(np.float32)
    ang = (pos[:, None] * inv[None, :]).astype(np.float32).astype(np.float64)
    cos, sin = np.cos(ang), np.sin(ang)
    for name, tab in (("cos_row", cos), ("sin_row", sin)):
        pad = np.zeros((3 * P, half))
        pad[:NT] = tab
        parts[name] = pad.reshape(3, P, half).transpose(1, 0, 2).reshape(P, 3 * half)
    d = i % DH % half
    parts["cos_T"] = cos[:, d].T
    parts["sin_T"] = sin[:, d].T * np.where(i % DH < half, -1.0, 1.0)[:, None]
    partner = i // DH * DH + (i % DH + half) % DH
    parts["swap"] = (i[:, None] == partner[None, :])
    return {k: np.asarray(v, np.float32) for k, v in parts.items()}


PARTS = constant_parts()
CONST_AT, CONST_N = {}, 0
for _name, _part in PARTS.items():
    CONST_AT[_name] = (CONST_N, CONST_N + _part.shape[1])
    CONST_N += _part.shape[1]

BLOCKS = [("kv", C_KV, 512, False), ("kv", C_KV + 512, KVW - 512, False), ("q", C_Q, 512, True),
          ("hf", C_HF, 512, True), ("hq", C_HQ, 512, True), ("hi", C_HI, 512, False),
          ("hg", C_HG, 512, False), ("ga", C_GA, 512, True), ("ga", C_GA + 512, 512, True),
          ("gb", C_GB, 512, True), ("gb", C_GB + 512, 512, True)]
NW = 3


def projection_groups():
    out = []
    for j, (kind, _, _, turned) in enumerate(BLOCKS):
        out += [(kind, j, n) for n in range(4 if turned else 3)]
        if kind == "hf":
            out += [("rot", j, n) for n in range(4)]
        if kind == "hq":
            out += [("kT", j, n) for n in range(2)]
    return out


GROUPS = projection_groups()
ON_DVE = ("q", "hi", "rot", "kT")
J_Q = [b[0] for b in BLOCKS].index("q")
NB = 5
LEVEL_AFTER = [n for n, g in enumerate(GROUPS) if g[0] in ("ga", "gb")][1::2][:len(LEVELS)]


class OwnSteps:

    def __init__(self, engine, semaphore):
        self.engine, self.semaphore, self.count, self.values = engine, semaphore, 0, {}

    def next(self, name):
        self.count += 1
        self.values.setdefault(name, []).append(self.count)
        return self.semaphore

    def wait(self, name, n):
        self.engine.wait_ge(self.semaphore, self.values[name][n - 1])

    def chain(self, name, start):
        def step(instruction, n=1):
            instruction.then_inc(self.next(name), 1)
            self.engine.wait_ge(self.semaphore, self.count)
        return step


def trunk_kernel(nc, ins, outs):
    with ExitStack() as ctx:
        ctx.enter_context(nc.allow_non_contiguous_dma(reason="small parameter tables"))

        def sb(name, shape, dt=F32):
            return ctx.enter_context(nc.sbuf_tensor(name, shape, dt))

        def sem(name):
            return ctx.enter_context(nc.semaphore(name))

        psum = [ctx.enter_context(nc.psum_tensor(f"bank{b}", [P, 512], F32)) for b in range(8)]

        gate_scratch = nc.dram_tensor("gate_scratch", [3, NS * G * HG], F32, kind="Internal").ap()

        const = sb("const", [P, CONST_N])

        def C(name, rows=P):
            a, b = CONST_AT[name]
            return const[0:rows, a:b]

        ident = C("ident")

        big = sb("big", [P, 24576])

        def part(t, at, shape):
            n = math.prod(shape)
            v = t[:, at:at + n]
            if len(shape) == 1:
                return v
            names = "abcdef"[:len(shape)]
            sizes = {k: m for k, m in zip(names[1:], shape[1:])}
            return v.rearrange(f"p ({' '.join(names)}) -> p {' '.join(names)}", **sizes)

        w_slot = [part(big, 4096 * s, [KD, 512]) for s in range(NW)]
        x_rows = part(big, 20480, [3, D])
        w1 = part(big, 12288, [2, LP, HID])
        pages = part(big, 20480, [2, 4, 2, 2, GD])
        XT = part(big, 0, [2, G * 4, 512])
        hidT = part(big, 8192, [2, 504])
        pair_rows = part(big, 9216, [2, 2, GD])
        XTp = part(big, 9728, [2, G, P])
        S0 = part(big, 12288, [DB, HH, DK])
        own_i = part(big, 16384, [2, DB, DK])
        khat = part(big, 18432, [3, 512])
        Sp = part(big, 19968, [2, 512])
        qe_own = part(big, 20992, [HH, DB, NS])
        S_decayed = part(big, 22016, [DB, DK])
        probs = part(big, 19968, [HG, 2, SEQ])
        probsT = part(big, 22016, [5, 512])
        slc_rows = [part(big, 12288 * s, [4, NPG, 2, GD]) for s in range(2)]
        win_rows = [part(big, 12288 * s + 8192, [4, 4, 2, GD]) for s in range(2)]
        w_pa = part(big, 0, [HG, D])
        w_pb = part(big, 4096, [HH, D])
        w_o = part(big, 8192, [KD, D])
        gu_slot = [part(big, 2 * D * k, [2 * DF]) for k in range(KD)]
        dn_slot = [part(big, 16384 + D * k, [D]) for k in range(KD)]

        xT = sb("xT", [P, KD * NT])
        xTv = part(xT, 0, [KD, NT])
        ckT = part(xT, 0, [DB, NCS])
        cv = part(xT, 504, [DB, GD])
        ckTp = part(xT, 1528, [16])
        cvp = part(xT, 1544, [GD])
        peT = part(xT, 1672, [2, LP])
        hT = xTv

        kv = sb("kv", [P, 3, KVW])
        kT = sb("kT", [P, 2, NT])
        gates = sb("gates", [P, 16 * NT])
        gatesT = part(gates, 0, [16, NT])
        qT = sb("qT", [P, 2, HG, NT])
        hi = sb("hi", [P, 3, 512])
        hg = sb("hg", [P, 3, 512])
        work = sb("work", [P, 6 * HH * NT])
        hq, hk, hb, hF, hqF, hkF = (part(work, n * HH * NT, [HH, NT]) for n in range(6))
        rope_t = part(work, 3 * HH * NT, [2, 2, 2, 32])
        rope_q = part(work, 4 * HH * NT, [NT])
        o_rows = part(work, 0, [3, 512])
        o_sq = part(work, 2 * HH * NT, [512])
        s_rows = part(work, 0, [1664])
        s_T = part(work, 1664, [4, 512])
        kt_stage = part(work, 3712, [2, 512])
        q_own = part(work, 4736, [2, 4, P])
        ln1 = part(kv[:, :, :].rearrange("p t n -> p (t n)"), 0, [2, D])
        h_rows = part(work, 0, [3, D])
        y_rows = part(work, 3 * D, [3, D])

        att = sb("att", [P, HH * NT])
        attv = [part(att, 0, [HH, P]), part(att, 512, [HH, P]), part(att, 1024, [HH, NS])]
        hgoT = part(att, 0, [HH, NT])
        nsaT = sb("nsaT", [P, HG, NT])
        nsa_flat = nsaT[:, :, :].rearrange("p h t -> p (h t)")
        att_t = [part(nsa_flat, 0, [HH, P]), part(nsa_flat, 512, [HH, P]), part(nsa_flat, 1024, [HH, NS])]
        small = sb("small", [P, 920])
        w2 = part(small, 0, [2, 2, DH])
        pe_bias = part(small, 256, [2, 2])
        lb_rows = part(small, 260, [2, HH])
        lb = part(small, 268, [HH])
        one_lb = part(small, 272, [HH])
        bgate = part(small, 276, [3, 3 * G * HG])
        sgate = part(small, 348, [2, 3])
        stat = part(small, 354, [6, 12])
        page_ids = ctx.enter_context(nc.sbuf_tensor("page_ids", [1, DB * NPG], I32))
        pick = part(small, 884, [15])
        drop = part(small, 899, [17])
        norm_w = part(small, 426, [DK])
        pe_rows = part(small, 554, [2, P])
        pc_rows = part(small, 810, [HG, NCP])
        ms = part(small, 870, [3 * HH])

        gu_pair = [part(big, 4 * DF * k, [2, 2 * DF]) for k in range(KD // 2)]
        dn_pair = [part(big, 16384 + 2 * D * k, [2, D]) for k in range(KD // 2)]
        w_router = part(small, 0, [KD, NE])
        b_router = part(small, 554, [NE])
        ln_sum, ln_sq = part(small, 590, [3]), part(small, 593, [3])
        top = part(small, 600, [3, 8])
        negtop = part(small, 624, [3])
        picked = part(small, 627, [3])
        over = part(small, 630, [5])
        logits, above, equal, ranks, select, gate, place = (part(nsa_flat, 96 * n, [3, NE]) for n in range(7))
        rounds_i = ctx.enter_context(nc.sbuf_tensor("rounds_i", [1, 1], I32))
        mixT = part(qT[:, :, :, :].rearrange("p r h n -> p (r h n)"), 0, [KD, NT])
        mix_t = part(hi[:, :, :].rearrange("p t n -> p (t n)"), 0, [2, 2, NT])
        ln2 = [part(t[:, :, :].rearrange("p t n -> p (t n)"), 0, [D]) for t in (hi, hg)]
        xg = part(xT, 0, [512])
        xe = part(gates, 0, [4, P])
        pgT = part(gates, 512, [3, P])
        g_lim, u_lim, sg, act_rows = (part(gates, 896 + 512 * n, [512]) for n in range(4))
        act_T = part(gates, 2944, [4, P])
        ye = part(gates, 3456, [512])
        pick_rows = part(gates, 3968, [3, CAP])
        pg = part(gates, 4160, [3, 2, CAP])
        gu_bias = part(kv[:, :, :].rearrange("p t n -> p (t n)"), 0, [2 * DF])
        dn_bias = part(att, 0, [D])

        x_loaded, wq_loaded = sem("x_loaded"), sem("wq_loaded")
        w_loaded = [sem(f"w_loaded{s}") for s in range(NW)]
        small_loaded = sem("small_loaded")
        ids_loaded = sem("ids_loaded")
        dve_own = sem("dve_own")
        x_turned, x_copied = sem("x_turned"), sem("x_copied")
        proj_done = sem("proj_done")
        bank_free = [sem(f"bank_free{b}") for b in range(NB)]
        kv_ready, stored = sem("kv_ready"), sem("stored")
        lb_diff, lb_sig, f_ready, logf_ready = sem("lb_diff"), sem("lb_sig"), sem("f_ready"), sem("logf_ready")
        diff_ready, decay_abs, decay_ready = sem("diff_ready"), sem("decay_abs"), sem("decay_ready")
        qf_ready, kf_ready = sem("qf_ready"), sem("kf_ready")
        level_done, level_masked, level_added = sem("level_done"), sem("level_masked"), sem("level_added")
        gates_ready = sem("gates_ready")
        page_loaded = [sem(f"page_loaded{s}") for s in range(2)]
        page_used = sem("page_used")
        xt_act, xt_dve, xt_turned = sem("xt_act"), sem("xt_dve"), sem("xt_turned")
        codes_done, codes_copied = sem("codes_done"), sem("codes_copied")
        hid_done, gelu_done, c_done, c_copied = sem("hid_done"), sem("gelu_done"), sem("c_done"), sem("c_copied")
        pairs_loaded = sem("pairs_loaded")
        cmp_rows_stored, states_stored = sem("cmp_rows_stored"), sem("states_stored")
        rows_loaded = [sem(f"rows_loaded{s}") for s in range(2)]
        q_own_ready, small_scores = sem("q_own_ready"), sem("small_scores")
        cneg_ready, cexp_done, cp_ready = sem("cneg_ready"), sem("cexp_done"), sem("cp_ready")
        imp_done = sem("imp_done")
        key_turned, key_copied, scores_done = sem("key_turned"), sem("key_copied"), sem("scores_done")
        rows_step, rows_act, neg_ready, exp_done = sem("rows_step"), sem("rows_act"), sem("neg_ready"), sem("exp_done")
        prob_ready, st_turned, st_copied, spv_done = sem("prob_ready"), sem("st_turned"), sem("st_copied"), sem("spv_done")
        snsa_copied = sem("snsa_copied")
        wout_loaded, wo_loaded, x_again, ln2_loaded = sem("wout_loaded"), sem("wo_loaded"), sem("x_again"), sem("ln2_loaded")
        ab_done, mix_ready, wo_done = sem("ab_done"), sem("mix_ready"), sem("wo_done")
        h_clear, ln_step, ln_sq_done, ln_rms = sem("h_clear"), sem("ln_step"), sem("ln_sq_done"), sem("ln_rms")
        h_ready = sem("h_ready")
        router_loaded, hT_turned, hT_copied, logits_done = sem("router_loaded"), sem("hT_turned"), sem("hT_copied"), sem("logits_done")
        ex_ready, select_ready, place_done, place_ready = sem("ex_ready"), sem("select_ready"), sem("place_done"), sem("place_ready")
        y_started = sem("y_started")
        gu_free, dn_free = sem("gu_free"), sem("dn_free")
        gu_loaded = [sem(f"gu_loaded{k}") for k in range(KD // 2)]
        dn_loaded = [sem(f"dn_loaded{k}") for k in range(KD // 2)]
        gu_bias_loaded, dn_bias_loaded = sem("gu_bias_loaded"), sem("dn_bias_loaded")
        pick_ready, pick_shifted, pg_ready = sem("pick_ready"), sem("pick_shifted"), sem("pg_ready")
        gathered, pg_turned, xe_copied, pgT_copied = sem("gathered"), sem("pg_turned"), sem("xe_copied"), sem("pgT_copied")
        xg_copied, xe_turned = sem("xg_copied"), sem("xe_turned")
        gu_done, g_ready, u_ready, sg_ready = sem("gu_done"), sem("g_ready"), sem("u_ready"), sem("sg_ready")
        ug_ready, act_ready = sem("ug_ready"), sem("act_ready")
        act_turned, act_copied, dn_done, ye_copied = sem("act_turned"), sem("act_copied"), sem("dn_done"), sem("ye_copied")
        comb_done, y_added = sem("comb_done"), sem("y_added")
        ln_var, negtop_ready, y_ready = sem("ln_var"), sem("negtop_ready"), sem("y_ready")
        eb_ready, kd_diff, kd_ready, scales_ready = sem("eb_ready"), sem("kd_diff"), sem("kd_ready"), sem("scales_ready")
        S0_loaded, khat_turned, khat_ready = sem("S0_loaded"), sem("khat_turned"), sem("khat_ready")
        gain_done, state_step, inter_done, qe_ready = sem("gain_done"), sem("state_step"), sem("inter_done"), sem("qe_ready")
        own_ready, sgain_done, sstate_step = sem("own_ready"), sem("sgain_done"), sem("sstate_step")
        o_done, o_copied, ms_ready, rms_ready = sem("o_done"), sem("o_copied"), sem("ms_ready"), sem("rms_ready")
        o_ready = sem("o_ready")
        hgo_turned, hgo_copied = sem("hgo_turned"), sem("hgo_copied")
        ps_done, ps_step, ps_act, pmax_ready = sem("ps_done"), sem("ps_step"), sem("ps_act"), sem("pmax_ready")
        pexp_done, pp_ready = sem("pexp_done"), sem("pp_ready")
        pt_turned, pt_copied, pv_done, nsa_copied = sem("pt_turned"), sem("pt_copied"), sem("pv_done"), sem("nsa_copied")
        state_p_stored = sem("state_p_stored")
        gscratch, sgate_loaded = sem("gscratch"), sem("sgate_loaded")
        forerun = {"pe": [(s_, 1) for s_ in (pg_turned, act_turned, dn_done)],
                   "act": [(s_, 1) for s_ in (sg_ready, act_copied)],
                   "dve": [(s_, 1) for s_ in (u_ready, ug_ready, act_ready)] + [(y_added, 6)]}

        def start_counts(eng, name):
            for s_, n in forerun[name]:
                eng.sem_inc(s_, n)

        block = ctx.enter_context(nc.Block())
        NG = len(GROUPS)

        def first_group(j):
            return min(n for n, g in enumerate(GROUPS) if g[1] >= j)

        def evacuated(eng, g):
            eng.wait_ge(bank_free[g % NB], g // NB + 1)

        def all_evacuated(eng):
            for g in range(NG - NB, NG):
                evacuated(eng, g)

        last_of = {}
        for n_, g_ in enumerate(GROUPS):
            last_of.setdefault(g_[0], []).append(n_)

        def copy_turned(copy, u, b4, jj, l, g, turns):
            if u < 2:
                return copy(XT[l * DH:(l + 1) * DH, :, 4 * g + b4, 2 * jj * P:2 * (jj + 1) * P],
                            psum[turns % 3][g * DH:(g + 1) * DH, :].rearrange("p (v n) -> p v n", v=2))
            return copy(XTp[l * DH:(l + 1) * DH, :, g, :],
                        psum[l][g * DH:(g + 1) * DH, 0:2 * P].rearrange("p (v n) -> p v n", v=2))

        def score(pe, s, n):
            b4, part_ = n % 12 // 3, n % 3
            pe.wait_ge(key_copied, n + 1)
            if b4 == 0 and s:
                pe.wait_ge(rows_step, 5)
                pe.wait_ge(rows_act, 1)
            pe.matmul(psum[1 + part_][:, :], q_own[:, 1, b4, :], kt_stage[:, n % 2, :],
                      start=(b4 == 0), stop=(b4 == 3), skip_group_check=True).then_inc(scores_done, 1)

        def rounds_of(eng):
            eng.wait_ge(place_ready, 2)
            return eng.value_load(rounds_i[0:1, 0:1], min_val=1, max_val=5)

        @block.sync
        def _(sp):
            sp.dma_start(x_rows[:, 0:2, :], ins["x_prompt"][0].rearrange("(t p) n -> p t n", p=P)).then_inc(x_loaded, 16)
            sp.dma_start(x_rows[0:NS, 2, :], ins["x_sample"].rearrange("b t n -> (b t) n")).then_inc(x_loaded, 16)
            sp.dma_start(const[:, :], ins["consts"]).then_inc(x_loaded, 16)

            def load_pages(b):
                for q in range(NPG):
                    page = sp.value_load(page_ids[0:1, b * NPG + q:b * NPG + q + 1], min_val=0, max_val=NPOOL - 1)
                    sp.dma_start(pages[64 * (q % 2):64 * (q % 2) + 64, b % 2, q // 2, :, :, :],
                                 ins["cache_cmp_kv"][0, bass.ds(page, 1)].rearrange("o (r l) v g d -> (o r) l v (g d)", l=2))\
                      .then_inc(page_loaded[b % 2], 16)

            for j, (_, c0, n, _) in enumerate(BLOCKS):
                if j == 2:
                    for r in range(2):
                        sp.dma_start(lb_rows[:, r, :], ins["hg_lb_logits"][r].rearrange("(h k) -> k h", k=DK)).then_inc(small_loaded, 16)
                    sp.dma_start(page_ids[:, :], ins["page_table"].rearrange("b q -> (b q)")[None, :]).then_inc(ids_loaded, 16)
                    for v, name in enumerate(("k", "v")):
                        sp.dma_start(w2[:, v, :, :], ins[f"w_c{name}2"][0].rearrange("(m p) d -> p m d", p=P)).then_inc(small_loaded, 16)
                        sp.dma_start(pe_rows[0:LP, v, :], ins[f"pe_c{name}"][0].rearrange("(a l) d -> a (l d)", l=2)).then_inc(small_loaded, 16)
                    sp.dma_start(norm_w, ins["hg_norm_w"].partition_broadcast(P).rearrange("p a n -> p (a n)")).then_inc(small_loaded, 16)
                if j >= NW:
                    sp.wait_ge(proj_done, first_group(j - NW + 1))
                if j == NW:
                    for v, name in enumerate(("k", "v")):
                        sp.dma_start(w1[:, v, :, :], ins[f"w_c{name}1"][0].rearrange("(a p) n -> p a n", p=P)).then_inc(small_loaded, 16)
                    sp.wait_ge(ids_loaded, 16)
                    sp.wait_ge(x_turned, 5)
                    load_pages(0)
                    load_pages(1)
                src = ins["w_in"][0, :, c0:c0 + n].rearrange("(k p) n -> p k n", p=P)
                if j == J_Q:
                    for g in range(G):
                        for h in range(HG):
                            sp.dma_start(w_slot[j % NW][:, :, (h * G + g) * DH:(h * G + g + 1) * DH],
                                         src[:, :, (g * HG + h) * DH:(g * HG + h + 1) * DH]).then_inc(wq_loaded, 16)
                else:
                    sp.dma_start(w_slot[j % NW][:, :, 0:n], src).then_inc(w_loaded[j % NW], 16)
            for b in range(2, DB):
                sp.wait_ge(page_used, b - 1)
                load_pages(b)
            sp.wait_ge(cmp_rows_stored, 16)
            sp.dma_start(pair_rows[:, :, :, :], outs["cmp_p"][0, 0].rearrange("(r l) v g d -> r l v (g d)", l=2)).then_inc(pairs_loaded, 16)
            sp.wait_ge(hid_done, 12)
            for b in range(DB):
                sp.dma_start(S0[:, b, :, :], ins["state_hgrn"][0, b].rearrange("h k v -> k h v")).then_inc(S0_loaded, 16)
            def load_rows(s):
                for b4 in range(4):
                    b = 4 * s + b4
                    for q in range(NPG):
                        page = sp.value_load(page_ids[0:1, b * NPG + q:b * NPG + q + 1], min_val=0, max_val=NPOOL - 1)
                        sp.dma_start(slc_rows[s][:, b4, q, :, :],
                                     ins["cache_slc_kv"][0, bass.ds(page, 1)].rearrange("o r v g d -> (o r) v (g d)")).then_inc(rows_loaded[s], 16)
                    sp.dma_start(win_rows[s][:, b4, :, :, :],
                                 ins["cache_win_kv"][0, b].rearrange("(j p) v g d -> p j v (g d)", p=P)).then_inc(rows_loaded[s], 16)

            sp.wait_ge(c_done, 6)
            load_rows(0)
            sp.wait_ge(pv_done, len(ITS))
            sp.wait_ge(states_stored, 16 * DB)
            load_rows(1)
            sp.wait_ge(spv_done, 1)
            for g in range(G):
                sp.dma_start(w_pa[g * DH:(g + 1) * DH, :, :],
                             ins["w_pa"][0, g * HG * DH:(g + 1) * HG * DH].rearrange("(h d) n -> d h n", d=DH)).then_inc(wout_loaded, 16)
            sp.dma_start(w_pb[:, :, :], ins["w_pb"][0].rearrange("(h d) n -> d h n", d=DK)).then_inc(wout_loaded, 16)
            sp.wait_ge(spv_done, 2)
            sp.dma_start(w_o[:, :, :], ins["w_o"][0].rearrange("(k p) n -> p k n", p=P)).then_inc(wo_loaded, 16)
            sp.wait_ge(snsa_copied, 4)
            sp.wait_ge(h_clear, 1)
            sp.dma_start(h_rows[:, 0:2, :], ins["x_prompt"][0].rearrange("(t p) n -> p t n", p=P)).then_inc(x_again, 16)
            sp.dma_start(h_rows[0:NS, 2, :], ins["x_sample"].rearrange("b t n -> (b t) n")).then_inc(x_again, 16)
            for n, name in enumerate(("ln1_g", "ln1_b")):
                sp.dma_start(ln1[:, n, :], ins[name].partition_broadcast(P).rearrange("p a n -> p (a n)")).then_inc(x_again, 16)
            sp.wait_ge(c_done, 6)
            sp.dma_start(w_router[:, :, :], ins["w_router"][0].rearrange("(k p) n -> p k n", p=P)).then_inc(router_loaded, 16)
            sp.dma_start(b_router, ins["b_router"].partition_broadcast(P).rearrange("p a n -> p (a n)")).then_inc(router_loaded, 16)
            sp.wait_ge(mix_ready, KD)
            for n, name in enumerate(("ln2_g", "ln2_b")):
                sp.dma_start(ln2[n], ins[name].partition_broadcast(P).rearrange("p a n -> p (a n)")).then_inc(ln2_loaded, 16)

            def load_gu(e, i, k):
                sp.wait_ge(gu_free, i * KD + 2 * k + 2)
                sp.dma_start(gu_pair[k], w_rows("w_gu", e, k)).then_inc(gu_loaded[k], 16)

            def load_dn(e, i, k):
                sp.wait_ge(dn_free, i * KD + 2 * k + 2)
                sp.dma_start(dn_pair[k], w_rows("w_dn", e, k)).then_inc(dn_loaded[k], 16)

            def w_rows(name, e, k):
                return ins[name][0, bass.ds(e, 1), 2 * k * P:(2 * k + 2) * P, :].rearrange("o (a p) n -> (o p) a n", p=P)

            for k in range(KD // 2):
                load_dn(0, 0, k)
            for k in range(KD // 2):
                load_gu(0, 0, k)
            sp.wait_ge(h_ready, 3)
            sp.dma_start(gu_bias[0:1, :], ins["b_gu"][0, 0:1, :]).then_inc(gu_bias_loaded, 16)
            sp.dma_start(dn_bias[0:1, :], ins["b_dn"][0, 0:1, :]).then_inc(dn_bias_loaded, 16)

            def load_expert(e, i):
                for k in range(KD // 2):
                    load_gu(e, i, k)
                sp.wait_ge(gu_done, i)
                sp.dma_start(gu_bias[0:1, :], ins["b_gu"][0, bass.ds(e, 1), :]).then_inc(gu_bias_loaded, 16)
                for k in range(KD // 2):
                    load_dn(e, i, k)
                sp.wait_ge(dn_done, i + 1)
                sp.dma_start(dn_bias[0:1, :], ins["b_dn"][0, bass.ds(e, 1), :]).then_inc(dn_bias_loaded, 16)

            with sp.Fori(1, NE) as e:
                load_expert(e, e)
            rounds = rounds_of(sp)
            with sp.If(rounds > 1):
                with sp.Fori(1, rounds) as r:
                    with sp.Fori(0, NE) as e:
                        load_expert(e, r * NE + e)

        @block.tensor
        def _(pe):
            pe.wait_ge(x_loaded, 48)
            for t in range(2):
                for h in range(2):
                    for k in range(4):
                        last = pe.transpose(psum[2 * t + h][:, k * P:(k + 1) * P],
                                            x_rows[:, t, (4 * h + k) * P:(4 * h + k + 1) * P], ident)
                    last.then_inc(x_turned, 1)
            for k in range(KD):
                last = pe.transpose(psum[4][:, k * NS:(k + 1) * NS], x_rows[0:NS, 2, k * P:(k + 1) * P], ident[0:NS, 0:NS])
            last.then_inc(x_turned, 1)
            pe.wait_ge(x_copied, 5)

            def level_scores(n):
                if n:
                    pe.wait_ge(qf_ready, n)
                    pe.wait_ge(kf_ready, n)
                    pe.wait_ge(level_masked, level_tiles_before(n))
                else:
                    pe.wait_ge(f_ready, HH * 2)
                q, k = (hqF, hkF) if n else (hq, hk)
                for t, (t0, m) in enumerate(TILES[:LEVEL_TILES[n]]):
                    for h in range(HH):
                        last = pe.matmul(psum[5 + t][0:m, h * m:(h + 1) * m], k[:, h, t0:t0 + m], q[:, h, t0:t0 + m],
                                         start=True, stop=True)
                last.then_inc(level_done, 1)

            for g, (kind, j, n) in enumerate(GROUPS):
                bank = psum[g % NB]
                if g >= NB:
                    evacuated(pe, g - NB)
                if g == first_group(j):
                    if j == J_Q:
                        pe.wait_ge(wq_loaded, 16 * G * HG)
                    else:
                        pe.wait_ge(w_loaded[j % NW], 16 * (j // NW + 1 - (j % NW == J_Q % NW and j > J_Q)))
                w = w_slot[j % NW]
                if kind == "rot":
                    evacuated(pe, last_of["q"][n])
                    last = pe.matmul(bank[:, 0:NT], C("swap"), qT[:, 0, n, :], start=True, stop=True)
                elif kind == "kT":
                    pe.wait_ge(kv_ready, 1)
                    for t, (t0, m) in enumerate(TILES):
                        last = pe.transpose(bank[:, t0:t0 + m], kv[0:m, t, (2 + 2 * n) * GD:(3 + 2 * n) * GD], ident[0:m, 0:m])
                elif BLOCKS[j][3]:
                    for k in range(KD):
                        last = pe.matmul(bank[:, 0:NT], w[:, k, n * P:(n + 1) * P], xTv[:, k, :],
                                         start=(k == 0), stop=(k == KD - 1))
                else:
                    t0, m = TILES[n]
                    cols = BLOCKS[j][2]
                    for k in range(KD):
                        last = pe.matmul(bank[0:m, 0:cols], xTv[:, k, t0:t0 + m], w[:, k, 0:cols],
                                         start=(k == 0), stop=(k == KD - 1))
                last.then_inc(proj_done, 1)
                if g in LEVEL_AFTER:
                    level_scores(LEVEL_AFTER.index(g))
            all_evacuated(pe)
            pe.wait_ge(small_loaded, 16 * 9)
            for v in range(2):
                last = pe.transpose(psum[3][:, v * LP:(v + 1) * LP], pe_rows[0:LP, v, :], ident[0:LP, 0:LP])
            last.then_inc(codes_done, 1)
            pe.wait_ge(codes_copied, 1)
            for v in range(2):
                for m in range(2):
                    for l in range(LP):
                        last = pe.matmul(psum[4][:, 2 * v + m:2 * v + m + 1], w1[:, v, l, m * P:(m + 1) * P],
                                         peT[:, v, l:l + 1], start=(l == 0), stop=(l == LP - 1))
            last.then_inc(codes_done, 1)
            pe.wait_ge(codes_copied, 2)
            turns = 0
            for u in range(3):
                if u < 2:
                    for b4 in range(4):
                        b = 4 * u + b4
                        pe.wait_ge(page_loaded[b % 2], 16 * NPG * (b // 2 + 1))
                        for jj in range(2):
                            for l in range(2):
                                if turns >= 3:
                                    pe.wait_ge(xt_act, turns - 2)
                                    pe.wait_ge(xt_dve, turns - 2)
                                for v in range(2):
                                    for j in range(2):
                                        last = pe.transpose(psum[turns % 3][:, (2 * v + j) * P:(2 * v + j + 1) * P],
                                                            pages[:, b % 2, 2 * jj + j, l, v, :], ident)
                                last.then_inc(xt_turned, 1)
                                turns += 1
                        pe.wait_ge(xt_turned, turns)
                        pe.sem_inc(page_used, 1)
                else:
                    pe.wait_ge(pairs_loaded, 16)
                    pe.wait_ge(xt_act, turns)
                    pe.wait_ge(xt_dve, turns)
                    for l in range(2):
                        for v in range(2):
                            last = pe.transpose(psum[l][:, v * P:(v + 1) * P], pair_rows[:, l, v, :], ident)
                        last.then_inc(xt_turned, 1)
                        turns += 1
                pe.wait_ge(xt_act, turns)
                pe.wait_ge(xt_dve, turns)
                nb, groups = (NCS, 8) if u < 2 else (NCP, 2)
                src = XT if u < 2 else XTp
                n_half = nb * groups // 2
                for v in range(2):
                    q = 2 * u + v
                    if q:
                        pe.wait_ge(c_copied, 2 * q)
                    for m in range(2):
                        out = psum[3 + m][:, 0:nb * groups]
                        for l in range(LP):
                            last = pe.matmul(out, w1[:, v, l, m * P:(m + 1) * P],
                                             src[:, v, :, l:l + 8 * (nb - 1) + 1:8], start=(l == 0), stop=(l == LP - 1))
                        last.then_inc(hid_done, 1)
                    pe.wait_ge(gelu_done, 2 * (q + 1))
                    if v == 0:
                        for g in range(G):
                            for m in range(2):
                                last = pe.matmul(psum[3][g * DH:(g + 1) * DH, 0:n_half], w2[:, 0, m, :],
                                                 hidT[:, m, g * n_half:(g + 1) * n_half], start=(m == 0), stop=(m == 1))
                    else:
                        for c in range(groups):
                            for m in range(2):
                                last = pe.matmul(psum[3][0:nb, c * DH:(c + 1) * DH], hidT[:, m, c * nb:(c + 1) * nb],
                                                 w2[:, 1, m, :], start=(m == 0), stop=(m == 1))
                    last.then_inc(c_done, 1)
            pe.wait_ge(scales_ready, 2)
            pe.wait_ge(level_added, level_tiles_before(len(LEVELS), 1))
            for e in last_of["hi"]:
                evacuated(pe, e)
            for t, (t0, m) in enumerate(TILES):
                for h in range(HH):
                    last = pe.transpose(psum[t][0:m, h * DK:(h + 1) * DK], hkF[:, h, t0:t0 + m], ident)
                last.then_inc(khat_turned, 1)
            for t, (t0, m) in enumerate(TILES):
                for h in range(HH):
                    pe.matmul(psum[5 + t][0:m, h * DK:(h + 1) * DK], attv[t][0:m, h, :], hi[0:m, t, h * DK:(h + 1) * DK],
                              start=(h == 0), stop=False, skip_group_check=True)
            for c in range(SEQ // CH):
                rows = slice(CH * (c % 2), CH * (c % 2) + CH)
                if c == 0:
                    pe.wait_ge(khat_ready, 3)
                    pe.wait_ge(c_copied, 12)
                if c >= 2:
                    pe.wait_ge(state_step, HH * (c - 1))
                for h in range(HH):
                    last = pe.matmul(psum[3 + c % 2][:, h * DK:(h + 1) * DK], khat[rows, c // 2, h * DK:(h + 1) * DK],
                                     hi[rows, c // 2, h * DK:(h + 1) * DK], start=True, stop=True)
                last.then_inc(gain_done, 1)
                if c:
                    pe.wait_ge(state_step, HH * c)
                    for h in range(HH):
                        last = pe.matmul(psum[5 + c // 2][rows, h * DK:(h + 1) * DK], hqF[:, h, CH * c:CH * (c + 1)],
                                         Sp[:, (c - 1) % 2, h * DK:(h + 1) * DK], start=False, stop=(c % 2 == 1),
                                         skip_group_check=True)
                    last.then_inc(inter_done, 1)
                    if c % 2:
                        pe.wait_ge(inter_done, c)
                        pe.sem_inc(o_done, 1)
            pe.wait_ge(S0_loaded, 16 * DB)
            pe.wait_ge(qe_ready, 2)
            for h in range(HH):
                for b in range(DB):
                    last = pe.matmul(psum[7][0:NS, h * DK:(h + 1) * DK], qe_own[:, h, b, :], S0[:, b, h, :],
                                     start=False, stop=(b == DB - 1), skip_group_check=True)
            last.then_inc(o_done, 1)
            for h in range(HH):
                pe.wait_ge(own_ready, h + 1)
                if h >= 2:
                    pe.wait_ge(sstate_step, 2 * (h - 1))
                for n in range(2):
                    last = pe.matmul(psum[2 * (h % 2) + n][:, :], khat[0:NS, 2, h * DK:(h + 1) * DK],
                                     own_i[0:NS, h % 2, 4 * n:4 * n + 4, :], start=True, stop=True)
                last.then_inc(sgain_done, 1)
            for t, (t0, m) in enumerate(TILES):
                pe.wait_ge(o_ready, t + 1)
                if t == 0:
                    pe.wait_ge(sstate_step, 8)
                for h in range(HH):
                    last = pe.transpose(psum[t][:, h * m:(h + 1) * m], o_rows[0:m, t, h * DK:(h + 1) * DK], ident[0:m, 0:m])
                last.then_inc(hgo_turned, 1)
            pe.wait_ge(hgo_copied, 3)
            turned = 0
            for it, (g, qt) in enumerate(ITS):
                rows = slice(g * DH, (g + 1) * DH)
                n_keys = (qt + 1) * P
                if it:
                    pe.wait_ge(ps_step, 5 * it)
                    pe.wait_ge(ps_act, PREV_ACT[it])
                for h in range(HG):
                    q = qT[rows, 1, h, qt * P:(qt + 1) * P]
                    for br in range(2):
                        pe.matmul(psum[h][:, br * SEQ:br * SEQ + n_keys], q, kT[rows, br, 0:n_keys], start=True, stop=True)
                for h in range(HG):
                    last = pe.matmul(psum[4][:, h * NCP:(h + 1) * NCP], qT[rows, 0, h, qt * P:(qt + 1) * P],
                                     ckTp[rows, 0:NCP], start=True, stop=True)
                last.then_inc(ps_done, 1)
                pe.wait_ge(pp_ready, 9 * (it + 1))
                blocks = [(br, kb) for br in range(2) for kb in range(qt + 1)] + [None]
                for i, blk in enumerate(blocks):
                    if turned >= 2:
                        pe.wait_ge(pt_copied, turned - 1)
                    out = psum[5 + turned % 2]
                    for h in range(HG):
                        if blk is None:
                            last = pe.transpose(out[0:NCP, h * P:(h + 1) * P], pc_rows[:, h, :], ident)
                        else:
                            br, kb = blk
                            last = pe.transpose(out[:, h * P:(h + 1) * P], probs[:, h, br, kb * P:(kb + 1) * P], ident)
                    last.then_inc(pt_turned, 1)
                    turned += 1
                pe.wait_ge(pt_copied, turned)
                if it:
                    pe.wait_ge(nsa_copied, it)
                for i, blk in enumerate(blocks):
                    if blk is None:
                        v, keys = cvp[0:NCP, rows], NCP
                    else:
                        v, keys = kv[:, blk[1], (3 + 2 * blk[0]) * GD + g * DH:(3 + 2 * blk[0]) * GD + (g + 1) * DH], P
                    last = pe.matmul(psum[7][rows, :], v, probsT[0:keys, i, :], start=(i == 0), stop=(blk is None))
                last.then_inc(pv_done, 1)
            for s in range(2):
                toks = slice(SEQ + 16 * s, SEQ + 16 * (s + 1))
                pe.wait_ge(q_own_ready, 4 * (s + 1))
                if s == 0:
                    pe.wait_ge(nsa_copied, len(ITS))
                    pe.wait_ge(ps_step, 5 * len(ITS))
                for b4 in range(4):
                    pe.matmul(psum[0][:, 0:NCS], q_own[:, 0, b4, :], ckT[:, 4 * s + b4, :], start=(b4 == 0), stop=(b4 == 3))
                for n in range(2):
                    for b4 in range(4):
                        last = pe.matmul(psum[0][:, 64 + NS * n:64 + NS * (n + 1)], q_own[:, 1, b4, :], kT[:, n, SEQ:NT],
                                         start=(b4 == 0), stop=(b4 == 3))
                last.then_inc(small_scores, 1)
                for b4 in range(4):
                    for part_ in range(3):
                        n = 12 * s + 3 * b4 + part_
                        if n >= 2:
                            pe.wait_ge(key_copied, n - 1)
                        if b4 == 0 and part_ == 0:
                            pe.wait_ge(rows_loaded[s], 16 * (NPG + 1) * 4)
                        for j in range(4):
                            rows = slc_rows[s][:, b4, 4 * part_ + j, 0, :] if part_ < 2 else win_rows[s][:, b4, j, 0, :]
                            last = pe.transpose(psum[4 + n % 2][:, j * P:(j + 1) * P], rows, ident)
                        last.then_inc(key_turned, 1)
                        if n % 12:
                            score(pe, s, n - 1)
                score(pe, s, 12 * s + 11)
                pe.wait_ge(cp_ready, s + 1)
                pe.matmul(psum[6][:, 0:NCS], C("same_group"), s_rows[:, 1600:1600 + NCS], start=True, stop=True).then_inc(imp_done, 1)
                pe.wait_ge(prob_ready, 3 * (s + 1))
                for q in range(4):
                    n = 4 * s + q
                    if n >= 2:
                        pe.wait_ge(st_copied, n - 1)
                    bank = psum[4 + n % 2]
                    if q < 3:
                        for j in range(4):
                            c0 = (4 * q + j) * P if q < 2 else 1056 + j * P
                            last = pe.transpose(bank[:, j * P:(j + 1) * P], s_rows[:, c0:c0 + P], ident)
                    else:
                        pe.transpose(bank[0:NS, 0:P], s_rows[:, PAST:PAST + NS], ident)
                        pe.transpose(bank[0:NS, P:2 * P], s_rows[:, 1568:1568 + NS], ident)
                        last = pe.transpose(bank[0:NCS, 2 * P:3 * P], s_rows[:, 1600:1600 + NCS], ident)
                    last.then_inc(st_turned, 1)
                pe.wait_ge(st_copied, 4 * (s + 1))
                out = psum[7][:, 0:P]
                if s:
                    pe.wait_ge(snsa_copied, 2)
                for n in range(2):
                    pe.matmul(out, kv[0:NS, 2, (3 + 2 * n) * GD:(4 + 2 * n) * GD], s_T[0:NS, 3, n * P:(n + 1) * P],
                              start=(n == 0), stop=False, skip_group_check=True)
                for b4 in range(4):
                    own = slice(b4 * 32, (b4 + 1) * 32)
                    pe.matmul(out[:, own], cv[0:NCS, 4 * s + b4, :], s_T[0:NCS, 3, 2 * P + b4 * 32:2 * P + (b4 + 1) * 32],
                              start=False, stop=False, skip_group_check=True)
                    for j in range(12):
                        v = slc_rows[s][:, b4, j, 1, :] if j < 8 else win_rows[s][:, b4, j - 8, 1, :]
                        last = pe.matmul(out[:, own], v, s_T[:, j // 4, (j % 4) * P + b4 * 32:(j % 4) * P + (b4 + 1) * 32],
                                         start=False, stop=(b4 == 3 and j == 11), skip_group_check=True)
                last.then_inc(spv_done, 1)
            pe.wait_ge(wout_loaded, 48)
            pe.wait_ge(snsa_copied, 4)
            pe.wait_ge(hgo_copied, 3)
            pe.wait_ge(rows_act, 2)
            for m in range(KD):
                if m >= 2:
                    pe.wait_ge(mix_ready, m - 1)
                cols = slice(m * P, (m + 1) * P)
                for n, (w, o) in enumerate(((w_pa, nsaT), (w_pb, hgoT))):
                    for h in range(4):
                        last = pe.matmul(psum[2 * (m % 2) + n][:, 0:NT], w[:, h, cols], o[:, h, :], start=(h == 0), stop=(h == 3))
                last.then_inc(ab_done, 1)
            pe.wait_ge(wo_loaded, 16)
            pe.wait_ge(mix_ready, KD)
            for i in range(6):
                t0, m = TILES[i // 2]
                for k in range(KD):
                    last = pe.matmul(psum[(4 + i) % 8][0:m, :], mixT[:, k, t0:t0 + m], w_o[:, k, (i % 2) * 512:(i % 2 + 1) * 512],
                                     start=(k == 0), stop=(k == KD - 1))
                last.then_inc(wo_done, 1)
            pe.wait_ge(wo_done, 6)
            pe.sem_inc(gu_free, KD)
            pe.sem_inc(dn_free, KD)
            pe.wait_ge(router_loaded, 32)
            for t, (t0, m) in enumerate(TILES):
                pe.wait_ge(h_ready, t + 1)
                for n in range(2):
                    i = 2 * t + n
                    if i >= 2:
                        pe.wait_ge(hT_copied, i - 1)
                    for k in range(4):
                        last = pe.transpose(psum[2 + i % 2][:, k * m:(k + 1) * m], h_rows[0:m, t, (4 * n + k) * P:(4 * n + k + 1) * P],
                                            ident[0:m, 0:m])
                    last.then_inc(hT_turned, 1)
            for t, (t0, m) in enumerate(TILES):
                pe.wait_ge(hT_copied, 2 * t + 2)
                for k in range(KD):
                    last = pe.matmul(psum[4 + t][0:m, 0:NE], hT[:, k, t0:t0 + m], w_router[:, k, :], start=(k == 0), stop=(k == KD - 1))
                last.then_inc(logits_done, 1)
            pe.wait_ge(select_ready, 1)
            for t in range(4):
                tiles = [u for u in range(min(t + 1, 3))]
                for u in tiles:
                    last = pe.matmul(psum[7][:, t * NE:(t + 1) * NE], C("before") if u == t else C("ones"), select[:, u, :],
                                     start=(u == 0), stop=(u == tiles[-1]))
            last.then_inc(place_done, 1)

            start_counts(pe, "pe")

            def gather(n):
                pe.wait_ge(pick_ready, n + 1)
                pe.wait_ge(pgT_copied, n if n is not 0 else 1)
                for t in range(3):
                    for half in range(2):
                        last = pe.matmul(psum[0][half * CAP:(half + 1) * CAP, :], pick_rows[:, t, :],
                                         h_rows[:, t, half * 512:(half + 1) * 512], start=(t == 0), stop=(t == 2),
                                         skip_group_check=True)
                last.then_inc(gathered, 1)

            def turn_rows(n):
                pe.wait_ge(xg_copied, n + 1)
                if n is not 0:
                    pe.wait_ge(xe_copied, n)
                for c in range(4):
                    last = pe.transpose(psum[1][:, c * P:(c + 1) * P], xg[:, c * P:(c + 1) * P], ident)
                last.then_inc(xe_turned, 1)

            def combine(i, t):
                pe.wait_ge(y_added, i * 6 + 2 * t + 6)
                for half in range(2):
                    rows = slice(half * CAP, (half + 1) * CAP)
                    last = pe.matmul(psum[6 + half][:, :], pgT[rows, t, :], ye[rows, :], start=True, stop=True)
                last.then_inc(comb_done, 1)

            def expert(i):
                pe.wait_ge(xe_copied, i + 1)
                pe.wait_ge(u_ready, i + 1)
                for k in range(KD):
                    if k % 2 == 0:
                        pe.wait_ge(gu_loaded[k // 2], i * 16 + 16)
                    for n in range(2):
                        for half in range(2):
                            c0 = n * DF + half * 512
                            last = pe.matmul(psum[2 + n][half * CAP:(half + 1) * CAP, :], xe[:, k % 4, (k // 4) * CAP:(k // 4 + 1) * CAP],
                                             gu_slot[k][:, c0:c0 + 512], start=(k == 0), stop=False, skip_group_check=True)
                    last.then_inc(gu_free, 1)
                pe.wait_ge(gu_bias_loaded, i * 16 + 16)
                for n in range(2):
                    for half in range(2):
                        c0 = n * DF + half * 512
                        last = pe.matmul(psum[2 + n][half * CAP:(half + 1) * CAP, :], C("ones", 1)[:, 0:CAP], gu_bias[0:1, c0:c0 + 512],
                                         start=False, stop=True, skip_group_check=True)
                last.then_inc(gu_done, 1)
                pe.wait_ge(ye_copied, i + 1)
                pe.wait_ge(pgT_copied, i + 1)
                combine(i, 0)
                gather(i + 1)
                pe.wait_ge(act_ready, i + 2)
                pe.wait_ge(act_copied, i + 1)
                for c in range(4):
                    last = pe.transpose(psum[4][:, c * P:(c + 1) * P], act_rows[:, c * P:(c + 1) * P], ident)
                last.then_inc(act_turned, 1)
                combine(i, 1)
                turn_rows(i + 1)
                pe.wait_ge(act_copied, i + 2)
                for k in range(KD):
                    if k % 2 == 0:
                        pe.wait_ge(dn_loaded[k // 2], i * 16 + 16)
                    for half in range(2):
                        last = pe.matmul(psum[5][half * CAP:(half + 1) * CAP, :], act_T[:, k % 4, (k // 4) * CAP:(k // 4 + 1) * CAP],
                                         dn_slot[k][:, half * 512:(half + 1) * 512], start=(k == 0), stop=False, skip_group_check=True)
                    last.then_inc(dn_free, 1)
                pe.wait_ge(dn_bias_loaded, i * 16 + 16)
                for half in range(2):
                    last = pe.matmul(psum[5][half * CAP:(half + 1) * CAP, :], C("ones", 1)[:, 0:CAP],
                                     dn_bias[0:1, half * 512:(half + 1) * 512], start=False, stop=True, skip_group_check=True)
                last.then_inc(dn_done, 1)
                combine(i, 2)
                pe.wait_ge(pg_ready, i + 1)
                pe.wait_ge(xg_copied, i + 2)
                for t in range(3):
                    last = pe.transpose(psum[0][:, t * P:(t + 1) * P], pg[:, t, :, :].rearrange("p a n -> p (a n)"), ident)
                last.then_inc(pg_turned, 1)

            rounds = rounds_of(pe)
            gather(0)
            turn_rows(0)
            with pe.Fori(0, rounds) as r:
                with pe.Fori(0, NE) as e:
                    expert(r * NE + e)
            last_one = rounds * NE
            pe.wait_ge(ye_copied, last_one + 1)
            pe.wait_ge(pgT_copied, last_one + 1)
            for t in range(3):
                combine(last_one, t)

        @block.scalar
        def _(act):
            def evacuate(kinds):
                for g, (kind, j, n) in enumerate(GROUPS):
                    if kind not in kinds:
                        continue
                    act.wait_ge(proj_done, g + 1)
                    bank = psum[g % NB]
                    m = TILES[n][1] if n < 3 else P
                    if kind == "kv":
                        c0, cols = BLOCKS[j][1] - C_KV, BLOCKS[j][2]
                        i = act.activation(kv[0:m, n, c0:c0 + cols], bank[0:m, 0:cols], ACT.Copy)
                    elif kind == "hg":
                        i = act.activation(hg[0:m, n, :], bank[0:m, :], ACT.Silu)
                    elif kind == "hq":
                        i = act.activation(hq[:, n, :], bank[:, 0:NT], ACT.Silu)
                    elif kind == "hf":
                        i = act.activation(hk[:, n, :], bank[:, 0:NT], ACT.Sigmoid)
                    i.then_inc(bank_free[g % NB], 1)

            def merge_gate(g):
                kind, j, n = GROUPS[g]
                act.wait_ge(proj_done, g + 1)
                at = (0 if kind == "ga" else 8) + (BLOCKS[j][1] - (C_GA if kind == "ga" else C_GB)) // P + n
                act.activation(gatesT[:, at, :], psum[g % NB][:, 0:NT], ACT.Copy).then_inc(bank_free[g % NB], 1)

            evacuate(("kv",))
            for g in last_of["kv"]:
                evacuated(act, g)
            act.activation(bgate[:, 0:2, :], kv[:, 0:2, 6 * GD:KVW], ACT.Sigmoid).then_inc(gates_ready, 1)
            act.activation(bgate[0:NS, 2, :], kv[0:NS, 2, 6 * GD:KVW], ACT.Sigmoid).then_inc(gates_ready, 1)
            evacuate(("hf",))
            act.wait_ge(lb_diff, 1)
            act.activation(lb, lb, ACT.Sigmoid).then_inc(lb_sig, 1)
            evacuate(("hq",))
            evacuate(("hg",))
            act.wait_ge(f_ready, 2 * HH)
            act.activation(hF[:, :, :], hF[:, :, :], ACT.Ln).then_inc(logf_ready, 1)
            merges = last_of["ga"] + last_of["gb"]
            done = 0
            for n in range(1, len(LEVELS)):
                while done < len(merges) and merges[done] <= LEVEL_AFTER[n - 1]:
                    merge_gate(merges[done])
                    done += 1
                act.wait_ge(diff_ready, n)
                act.activation(hF[:, :, :], hF[:, :, :], ACT.Abs).then_inc(decay_abs, 1)
                act.wait_ge(decay_abs, n)
                act.activation(hF[:, :, :], hF[:, :, :], ACT.Exp, scale=-1.0).then_inc(decay_ready, 1)
            while done < len(merges):
                merge_gate(merges[done])
                done += 1
            for g in merges:
                evacuated(act, g)
            act.activation(gates[:, :], gates[:, :], ACT.Sigmoid).then_inc(gates_ready, 1)
            act.wait_ge(qf_ready, 6)
            act.wait_ge(kf_ready, 6)
            act.activation(hF[:, :, :], hb[:, :, :], ACT.Exp).then_inc(eb_ready, 1)
            act.wait_ge(kd_diff, 2)
            act.activation(hkF[:, :, :], hkF[:, :, :], ACT.Exp).then_inc(kd_ready, 1)
            turns = 0
            for u in range(3):
                if u == 1:
                    act.wait_ge(hid_done, 4)
                for b4 in range(4 if u < 2 else 1):
                    for jj in range(2 if u < 2 else 1):
                        for l in range(2):
                            act.wait_ge(xt_turned, turns + 1)
                            copy_turned(lambda o, i: act.activation(o, i, ACT.Copy), u, b4, jj, l, 0, turns).then_inc(xt_act, 1)
                            turns += 1
                nb = NCS * 8 if u < 2 else NCP * 2
                for v in range(2):
                    q = 2 * u + v
                    if q:
                        act.wait_ge(c_done, q)
                    else:
                        act.wait_ge(codes_copied, 2)
                    for m in range(2):
                        act.wait_ge(hid_done, 2 * q + m + 1)
                        act.activation(hidT[:, m, 0:nb], psum[3 + m][:, 0:nb], ACT.Gelu_apprx_tanh,
                                       bias=pe_bias[:, v, m:m + 1]).then_inc(gelu_done, 1)
            for t, (t0, m) in enumerate(TILES):
                act.wait_ge(o_done, t + 1)
                act.activation(o_rows[0:m, t, :], psum[5 + t][0:m, :], ACT.Copy).then_inc(o_copied, 1)
            act.wait_ge(ms_ready, 3)
            act.activation(ms[:, 0:3 * HH], ms[:, 0:3 * HH], ACT.Sqrt).then_inc(rms_ready, 1)
            copied = 0
            for it, (g, qt) in enumerate(ITS):
                act.wait_ge(ps_done, it + 1)
                if qt:
                    for h in range(HG):
                        act.wait_ge(ps_step, 5 * it + h + 1)
                        act.activation(probs[:, h, :, 0:P], psum[h][:, :].rearrange("p (b n) -> p b n", b=2)[:, :, 0:P],
                                       ACT.Copy).then_inc(ps_act, 1)
                act.wait_ge(pmax_ready, it + 1)
                for h in range(HG):
                    for br in range(2):
                        c = 2 * h + br
                        act.activation(probs[:, h, br, 0:(qt + 1) * P], probs[:, h, br, 0:(qt + 1) * P], ACT.Exp,
                                       bias=stat[:, 0, c:c + 1], scale=SCALE, accum_out=stat[:, 1, c:c + 1]).then_inc(pexp_done, 1)
                for h in range(HG):
                    act.activation(pc_rows[:, h, :], pc_rows[:, h, :], ACT.Exp, bias=stat[:, 0, 8 + h:9 + h],
                                   scale=SCALE, accum_out=stat[:, 1, 8 + h:9 + h]).then_inc(pexp_done, 1)
                n = 2 * (qt + 1) + 1
                for i in range(n):
                    keys = P if i < n - 1 else NCP
                    act.wait_ge(pt_turned, copied + 1)
                    act.activation(probsT[0:keys, i, :], psum[5 + copied % 2][0:keys, :], ACT.Copy).then_inc(pt_copied, 1)
                    copied += 1
            def copy_key(n):
                act.wait_ge(key_turned, n + 1)
                if n >= 2:
                    act.wait_ge(scores_done, n - 1)
                act.activation(kt_stage[:, n % 2, :], psum[4 + n % 2][:, :], ACT.Copy).then_inc(key_copied, 1)

            for s in range(2):
                if s:
                    act.wait_ge(st_copied, 4)
                for n in range(3):
                    copy_key(12 * s + n)
                act.wait_ge(cneg_ready, s + 1)
                act.activation(s_rows[:, 1600:1600 + NCS], s_rows[:, 1600:1600 + NCS], ACT.Exp, bias=stat[:, 3, 0:1],
                               scale=SCALE, accum_out=stat[:, 3, 1:2]).then_inc(cexp_done, 1)
                for n in range(3, 12):
                    copy_key(12 * s + n)
                act.wait_ge(scores_done, 12 * (s + 1))
                act.activation(s_rows[:, 1056 + DT:1568], psum[3][:, DT:WIN], ACT.Copy).then_inc(rows_act, 1)
                act.wait_ge(neg_ready, s + 1)
                for n, (a, b) in enumerate(((0, 1056), (1056, 1600))):
                    act.activation(s_rows[:, a:b], s_rows[:, a:b], ACT.Exp, bias=stat[:, 3, 4 + n:5 + n], scale=SCALE,
                                   accum_out=stat[:, 3, 6 + n:7 + n]).then_inc(exp_done, 1)
                for q in range(4):
                    n = 4 * s + q
                    act.wait_ge(st_turned, n + 1)
                    if q < 3:
                        act.activation(s_T[:, q, :], psum[4 + n % 2][:, :], ACT.Copy).then_inc(st_copied, 1)
                    else:
                        act.activation(s_T[0:NS, q, 0:2 * P], psum[4 + n % 2][0:NS, 0:2 * P], ACT.Copy)
                        act.activation(s_T[0:NCS, q, 2 * P:3 * P], psum[4 + n % 2][0:NCS, 2 * P:3 * P], ACT.Copy).then_inc(st_copied, 1)
            def norm_parts(rows, scratch, n):
                for t, (t0, m) in enumerate(TILES):
                    act.wait_ge(ln_step, 9 * n + 3 * t + 3)
                    act.activation(scratch[0:m, t, :], rows[0:m, t, :], ACT.Square, accum_out=ln_sq[0:m, t:t + 1]).then_inc(ln_sq_done, 1)
                for t, (t0, m) in enumerate(TILES):
                    act.wait_ge(ln_var, 3 * n + t + 1)
                    act.activation(ln_sq[0:m, t:t + 1], ln_sq[0:m, t:t + 1], ACT.Sqrt).then_inc(ln_rms, 1)

            norm_parts(h_rows, y_rows, 0)
            for t, (t0, m) in enumerate(TILES):
                for n in range(2):
                    i = 2 * t + n
                    act.wait_ge(hT_turned, i + 1)
                    act.activation(hT[:, 4 * n:4 * n + 4, t0:t0 + m], psum[2 + i % 2][:, 0:4 * m].rearrange("p (k n) -> p k n", k=4),
                                   ACT.Copy).then_inc(hT_copied, 1)
            act.wait_ge(negtop_ready, 1)
            for t in range(3):
                act.activation(gate[:, t, :], logits[:, t, :], ACT.Exp, bias=negtop[:, t:t + 1]).then_inc(ex_ready, 1)
            for t in range(3):
                act.activation(y_rows[:, t, :], h_rows[:, t, :], ACT.Copy, scale=ALPHA).then_inc(y_started, 1)

            start_counts(act, "act")

            def take_rows(n):
                act.wait_ge(gathered, n + 1)
                if n is not 0:
                    act.wait_ge(xe_turned, n)
                act.activation(xg, psum[0][:, :], ACT.Copy).then_inc(xg_copied, 1)

            def take_turned(n):
                act.wait_ge(xe_turned, n + 1)
                if n is not 0:
                    act.wait_ge(gu_done, n)
                act.activation(xe, psum[1][:, :].rearrange("p (c n) -> p c n", c=4), ACT.Copy).then_inc(xe_copied, 1)

            def expert(i):
                act.wait_ge(g_ready, i + 1)
                act.wait_ge(act_ready, i + 1)
                act.activation(sg, g_lim, ACT.Sigmoid, scale=1.702).then_inc(sg_ready, 1)
                take_rows(i + 1)
                act.wait_ge(act_turned, i + 2)
                act.wait_ge(dn_done, i + 1)
                act.activation(act_T, psum[4][:, :].rearrange("p (c n) -> p c n", c=4), ACT.Copy).then_inc(act_copied, 1)
                take_turned(i + 1)
                act.wait_ge(dn_done, i + 2)
                act.wait_ge(comb_done, i * 3 + 3)
                act.activation(ye, psum[5][:, :], ACT.Copy).then_inc(ye_copied, 1)
                act.wait_ge(pg_turned, i + 2)
                act.activation(pgT, psum[0][:, 0:3 * P].rearrange("p (t n) -> p t n", t=3), ACT.Copy).then_inc(pgT_copied, 1)

            rounds = rounds_of(act)
            take_rows(0)
            take_turned(0)
            with act.Fori(0, rounds) as r:
                with act.Fori(0, NE) as e:
                    expert(r * NE + e)
            norm_parts(y_rows, h_rows, 1)

        @block.gpsimd
        def _(pool):
            pool.wait_ge(kv_ready, 1)
            n_stored = 0
            for s, name in enumerate(("cmp", "slc", "win")):
                c0 = s * 2 * GD
                pool.dma_start(outs[f"{name}_p"].rearrange("a b (t p) v g d -> p (a b t) (v g d)", p=P),
                               kv[:, 0:2, c0:c0 + 2 * GD]).then_inc(stored if s else cmp_rows_stored, 16)
                o = outs[f"{name}_s"]
                if name == "win":
                    pool.dma_start(o[0, :, 0:WIN - DT].rearrange("b r v g d -> b (r v g d)"),
                                   ins["cache_win_kv"][0, :, DT:WIN].rearrange("b r v g d -> b (r v g d)")).then_inc(stored, 16)
                    for b in range(DB):
                        pool.dma_start(o[0, b, WIN - DT:WIN].rearrange("r v g d -> r (v g d)"),
                                       kv[b * DT:(b + 1) * DT, 2, c0:c0 + 2 * GD]).then_inc(stored, 16)
                    n_stored += 2 + DB
                else:
                    pool.dma_start(o.rearrange("a b t v g d -> (a b t) (v g d)"), kv[0:NS, 2, c0:c0 + 2 * GD]).then_inc(stored, 16)
                    n_stored += 1 + (s > 0)
            for n in range(1, len(LEVELS)):
                pool.wait_ge(decay_ready, n)
                pool.wait_ge(level_done, n)
                pool.tensor_tensor(hkF[:, :, :], hk[:, :, :], hF[:, :, :], ALU.mult).then_inc(kf_ready, 1)
            pool.wait_ge(gates_ready, 2)
            pool.dma_start(gate_scratch.rearrange("c (t x) -> t c x", x=G * HG),
                           bgate[0:NS, 2, :].rearrange("p (c x) -> p c x", c=3)).then_inc(gscratch, 16)
            pool.wait_ge(gscratch, 16)
            for s in range(2):
                pool.dma_start(sgate[:, s, :], gate_scratch[:, s * P:(s + 1) * P].rearrange("c r -> r c")).then_inc(sgate_loaded, 16)
            pool.wait_ge(state_step, HH * 4)
            pool.dma_start(outs["state_p"][0, 0].rearrange("h k v -> k h v"),
                           Sp[:, 1, :].rearrange("p (h v) -> p h v", h=HH)).then_inc(state_p_stored, 16)
            pool.wait_ge(sstate_step, 2 * HH)
            for b in range(DB):
                pool.dma_start(outs["state_s"][0, b].rearrange("h k v -> k h v"), S0[:, b, :, :]).then_inc(states_stored, 16)
            def expert(e, i):
                pool.wait_ge(pick_ready, i + 1)
                pool.wait_ge(pg_turned, i + 1)
                for half in range(2):
                    last = pool.tensor_tensor(pg[:, :, half, :], pick_rows, gate[:, :, bass.ds(e, 1)].broadcast_to([P, 3, CAP]), ALU.mult)
                last.then_inc(pg_ready, 1)

            rounds = rounds_of(pool)
            with pool.Fori(0, rounds) as r:
                with pool.Fori(0, NE) as e:
                    expert(e, r * NE + e)
            for t, (t0, m) in enumerate(TILES):
                pool.wait_ge(y_ready, t + 1)
                if t < 2:
                    pool.dma_start(outs["y_p"][0, t0:t0 + m, :], y_rows[:, t, :]).then_inc(stored, 16)
                else:
                    pool.dma_start(outs["y_s"].rearrange("b t n -> (b t) n"), y_rows[0:NS, 2, :]).then_inc(stored, 16)
            n_stored += 3


            pool.wait_ge(stored, 16 * n_stored)
            pool.wait_ge(cmp_rows_stored, 16)
            pool.wait_ge(states_stored, 16 * DB)
            pool.wait_ge(state_p_stored, 16)

        @block.vector
        def _(dve):
            own = OwnSteps(dve, dve_own)
            for t in range(2):
                for h in range(2):
                    dve.wait_ge(x_turned, 2 * t + h + 1)
                    dve.tensor_copy(xTv[:, 4 * h:4 * h + 4, t * P:(t + 1) * P],
                                    psum[2 * t + h][:, :].rearrange("p (k n) -> p k n", k=4)).then_inc(x_copied, 1)
            dve.wait_ge(x_turned, 5)
            dve.tensor_copy(xTv[:, :, SEQ:NT], psum[4][:, 0:KD * NS].rearrange("p (k n) -> p k n", k=KD)).then_inc(x_copied, 1)

            def rope_rows():
                steps = 0
                for rows, t0, nt in ((P, 0, 2), (NS, 2, 1)):
                    cos = C("cos_row", rows).rearrange("p (t d) -> p t d", t=3)[:, t0:t0 + nt, :]
                    sin = C("sin_row", rows).rearrange("p (t d) -> p t d", t=3)[:, t0:t0 + nt, :]
                    for s in (2, 4):
                        for g in range(G):
                            c0 = s * GD + g * DH
                            x1 = kv[0:rows, t0:t0 + nt, c0:c0 + 32]
                            x2 = kv[0:rows, t0:t0 + nt, c0 + 32:c0 + 64]
                            u1 = rope_t[0:rows, g, 0, 0:nt, :]
                            u2 = rope_t[0:rows, g, 1, 0:nt, :]
                            if steps:
                                own.wait("rope_step", steps)
                            dve.tensor_tensor(u1, x1, sin, ALU.mult).then_inc(own.next("rope_step"), 1)
                            dve.tensor_tensor(u2, x2, sin, ALU.mult).then_inc(own.next("rope_step"), 1)
                            own.wait("rope_step", steps + 2)
                            dve.tensor_tensor(x1, x1, cos, ALU.mult).then_inc(own.next("rope_step"), 1)
                            dve.tensor_tensor(x2, x2, cos, ALU.mult).then_inc(own.next("rope_step"), 1)
                            own.wait("rope_step", steps + 4)
                            dve.tensor_tensor(x1, x1, u2, ALU.subtract).then_inc(own.next("rope_step"), 1)
                            dve.tensor_tensor(x2, x2, u1, ALU.add).then_inc(own.next("rope_step"), 1)
                            steps += 6
                own.wait("rope_step", steps)
                dve.sem_inc(kv_ready, 1)
                return steps

            for e in last_of["kv"]:
                evacuated(dve, e)
            dve.wait_ge(x_loaded, 48)
            rope_steps = rope_rows()

            def evacuate(kinds):
                for g, (kind, j, n) in enumerate(GROUPS):
                    if kind not in kinds:
                        continue
                    dve.wait_ge(proj_done, g + 1)
                    bank = psum[g % NB]
                    if kind == "q":
                        i = dve.tensor_copy(qT[:, 0, n, :], bank[:, 0:NT])
                    elif kind == "hi":
                        m = TILES[n][1]
                        i = dve.tensor_copy(hi[0:m, n, :], bank[0:m, :])
                    elif kind == "kT":
                        i = dve.tensor_copy(kT[:, n, :], bank[:, 0:NT])
                    else:
                        evacuated(dve, last_of["q"][n])
                        if n:
                            evacuated(dve, last_of["rot"][n - 1])
                        dve.tensor_tensor(qT[:, 1, n, :], bank[:, 0:NT], C("sin_T"), ALU.mult).then_inc(own.next("rope_step"), 1)
                        dve.tensor_tensor(rope_q, qT[:, 0, n, :], C("cos_T"), ALU.mult).then_inc(own.next("rope_step"), 1)
                        own.wait("rope_step", rope_steps + 2 * (n + 1))
                        i = dve.tensor_tensor(qT[:, 1, n, :], qT[:, 1, n, :], rope_q, ALU.add)
                    i.then_inc(bank_free[g % NB], 1)

            evacuate(("q",))
            dve.wait_ge(small_loaded, 16 * 9)
            dve.tensor_tensor(lb, lb_rows[:, 0, :], lb_rows[:, 1, :], ALU.subtract).then_inc(lb_diff, 1)
            evacuate(("rot",))
            evacuate(("kT",))
            evacuate(("hi",))
            dve.wait_ge(lb_sig, 1)
            dve.tensor_scalar(one_lb, lb, -1.0, 1.0, ALU.mult, ALU.add).then_inc(own.next("hg_step"), 1)
            own.wait("hg_step", 1)
            for h in range(HH):
                evacuated(dve, last_of["hf"][h])
                dve.tensor_scalar(hF[:, h, :], hk[:, h, :], one_lb[:, h:h + 1], lb[:, h:h + 1], ALU.mult, ALU.add).then_inc(f_ready, 1)
            for h in range(HH):
                dve.wait_ge(f_ready, h + 1)
                dve.tensor_scalar(hk[:, h, :], hF[:, h, :], -1.0, 1.0, ALU.mult, ALU.add).then_inc(f_ready, 1)
            dve.wait_ge(logf_ready, 1)
            for h in range(HH):
                dve.tensor_tensor_scan(hb[:, h, :], C("carry"), hF[:, h, :], 0.0, ALU.mult, ALU.add).then_inc(own.next("hg_step"), 1)
            own.wait("hg_step", 1 + HH)

            def half_diff(n):
                lv = LEVELS[n]
                if n > 1:
                    dve.wait_ge(qf_ready, n - 1)
                    dve.wait_ge(kf_ready, n - 1)
                if 2 * lv <= 32:
                    b = hb.rearrange("p h (c u) -> p (h c) u", u=2 * lv)
                    o = hF.rearrange("p h (c u) -> p (h c) u", u=2 * lv)
                    dve.tensor_tensor(o, b, b[:, :, lv - 1:lv].broadcast_to(list(b.shape)), ALU.subtract).then_inc(diff_ready, 1)
                else:
                    b = hb[:, :, 0:SEQ].rearrange("p h (c u) -> p h c u", u=2 * lv)
                    o = hF[:, :, 0:SEQ].rearrange("p h (c u) -> p h c u", u=2 * lv)
                    dve.tensor_tensor(o, b, b[:, :, :, lv - 1:lv].broadcast_to(list(b.shape)), ALU.subtract).then_inc(diff_ready, 1)

            def add_level(n):
                dve.wait_ge(level_done, n + 1)
                mask = C("ident") if n == 0 else C(f"level{LEVELS[n]}")
                for t, (t0, m) in enumerate(TILES[:LEVEL_TILES[n]]):
                    if n > 1:
                        dve.wait_ge(level_added, level_tiles_before(n - 1, 1) + t + 1)
                    dst = attv[t] if n == 0 else att_t[t]
                    dve.tensor_tensor(dst[0:m], psum[5 + t][0:m, 0:HH * m].rearrange("p (h t) -> p h t", h=HH),
                                      mask[0:m, 0:m].unsqueeze(1).broadcast_to([m, HH, m]), ALU.mult).then_inc(level_masked, 1)
                if n:
                    for t, (t0, m) in enumerate(TILES[:LEVEL_TILES[n]]):
                        dve.wait_ge(level_masked, level_tiles_before(n) + t + 1)
                        if n > 1:
                            dve.wait_ge(level_added, level_tiles_before(n - 1, 1) + t + 1)
                        dve.tensor_tensor(attv[t][0:m], attv[t][0:m], att_t[t][0:m], ALU.add).then_inc(level_added, 1)

            half_diff(1)
            for n in range(1, len(LEVELS)):
                dve.wait_ge(decay_ready, n)
                dve.wait_ge(level_done, n)
                dve.tensor_tensor(hqF[:, :, :], hq[:, :, :], hF[:, :, :], ALU.mult).then_inc(qf_ready, 1)
                if n + 1 < len(LEVELS):
                    half_diff(n + 1)
                add_level(n - 1)
            add_level(len(LEVELS) - 1)
            def chunks(a):
                return (a[:, :, 0:SEQ].rearrange("p h (c u) -> p h c u", u=CH),
                        a[:, :, SEQ:NT].rearrange("p h (c u) -> p h c u", u=DT))

            dve.wait_ge(level_done, len(LEVELS))
            for o, b in zip(chunks(hkF), chunks(hb)):
                n = b.shape[3]
                dve.tensor_tensor(o, b[:, :, :, n - 1:n].broadcast_to(list(b.shape)), b, ALU.subtract).then_inc(kd_diff, 1)

            def hgrn_scales():
                dve.wait_ge(eb_ready, 1)
                dve.tensor_tensor(hqF[:, :, :], hq[:, :, :], hF[:, :, :], ALU.mult).then_inc(scales_ready, 1)
                dve.wait_ge(kd_ready, 1)
                dve.tensor_tensor(hkF[:, :, :], hkF[:, :, :], hk[:, :, :], ALU.mult).then_inc(scales_ready, 1)
                for t, (t0, m) in enumerate(TILES):
                    evacuated(dve, last_of["hg"][t])
                    v = hg[0:m, t, :].rearrange("p (h n) -> p h n", h=HH)
                    dve.tensor_tensor(v, v, norm_w[0:m].unsqueeze(1).broadcast_to([m, HH, DK]), ALU.mult).then_inc(scales_ready, 1)

            dve.wait_ge(codes_done, 1)
            dve.tensor_copy(peT, psum[3][:, 0:2 * LP].rearrange("p (v l) -> p v l", v=2)).then_inc(codes_copied, 1)
            dve.wait_ge(codes_done, 2)
            dve.tensor_copy(pe_bias, psum[4][:, 0:4].rearrange("p (v m) -> p v m", v=2)).then_inc(codes_copied, 1)
            turns = 0
            for u in range(3):
                if u == 1:
                    dve.wait_ge(hid_done, 4)
                for b4 in range(4 if u < 2 else 1):
                    for jj in range(2 if u < 2 else 1):
                        for l in range(2):
                            dve.wait_ge(xt_turned, turns + 1)
                            copy_turned(dve.tensor_copy, u, b4, jj, l, 1, turns).then_inc(xt_dve, 1)
                            turns += 1
                if u == 0:
                    hgrn_scales()
                for v in range(2):
                    dve.wait_ge(c_done, 2 * u + v + 1)
                    if v == 0:
                        for g in range(G):
                            rows = slice(g * DH, (g + 1) * DH)
                            if u < 2:
                                i = dve.tensor_copy(ckT[rows, 4 * u:4 * u + 4, :],
                                                    psum[3][rows, 0:4 * NCS].rearrange("p (b n) -> p b n", b=4))
                            else:
                                i = dve.tensor_copy(ckTp[rows, 0:NCP], psum[3][rows, 0:NCP])
                            i.then_inc(c_copied, 1)
                    else:
                        for g in range(G):
                            if u < 2:
                                i = dve.tensor_copy(cv[0:NCS, 4 * u:4 * u + 4, g * DH:(g + 1) * DH],
                                                    psum[3][0:NCS, g * 256:(g + 1) * 256].rearrange("p (b d) -> p b d", b=4))
                            else:
                                i = dve.tensor_copy(cvp[0:NCP, g * DH:(g + 1) * DH], psum[3][0:NCP, g * DH:(g + 1) * DH])
                            i.then_inc(c_copied, 1)
            for t, (t0, m) in enumerate(TILES):
                dve.wait_ge(khat_turned, t + 1)
                dve.tensor_copy(khat[0:m, t, :], psum[t][0:m, :]).then_inc(khat_ready, 1)
            dve.wait_ge(khat_turned, 3)
            dve.memset(qe_own[:, :, :, :], 0.0).then_inc(qe_ready, 1)
            dve.wait_ge(qe_ready, 1)
            for h in range(HH):
                for b in range(DB):
                    i = dve.tensor_copy(qe_own[:, h, b, b * DT:(b + 1) * DT], hqF[:, h, SEQ + b * DT:SEQ + (b + 1) * DT])
            i.then_inc(qe_ready, 1)

            def own_rows(h):
                if h >= 2:
                    dve.wait_ge(sgain_done, h - 1)
                dve.tensor_tensor(own_i[0:NS, h % 2, :, :],
                                  hi[0:NS, 2, h * DK:(h + 1) * DK].unsqueeze(1).broadcast_to([NS, DB, DK]),
                                  C("own_batch", NS).unsqueeze(2).broadcast_to([NS, DB, DK]), ALU.mult).then_inc(own_ready, 1)

            for c in range(SEQ // CH):
                dve.wait_ge(gain_done, c + 1)
                if c:
                    dve.wait_ge(state_step, HH * c)
                if c >= 2:
                    dve.wait_ge(inter_done, c - 1)
                for h in range(HH):
                    cols = slice(h * DK, (h + 1) * DK)
                    if c == 0:
                        i = dve.tensor_copy(Sp[:, 0, cols], psum[3][:, cols])
                    else:
                        e = CH * (c + 1) - 1
                        i = dve.scalar_tensor_tensor(out=Sp[:, c % 2, cols], in0=Sp[:, (c - 1) % 2, cols], scalar=hF[:, h, e:e + 1],
                                                     in1=psum[3 + c % 2][:, cols], op0=ALU.mult, op1=ALU.add)
                    i.then_inc(state_step, 1)
                if c < 2:
                    own_rows(c)

            def square(t):
                m = TILES[t][1]
                dve.wait_ge(o_copied, t + 1)
                if t:
                    own.wait("o_step", 2 * t)
                dve.tensor_tensor(o_sq[0:m, :], o_rows[0:m, t, :], o_rows[0:m, t, :], ALU.mult).then_inc(own.next("o_step"), 1)
                own.wait("o_step", 2 * t + 1)
                dve.tensor_reduce(ms[0:m, HH * t:HH * (t + 1)], o_sq[0:m, :].rearrange("p (h n) -> p h n", h=HH),
                                  AXX, ALU.add).then_inc(own.next("o_step"), 1)
                own.wait("o_step", 2 * t + 2)
                dve.tensor_scalar(ms[0:m, HH * t:HH * (t + 1)], ms[0:m, HH * t:HH * (t + 1)], 1.0 / DK, RMS_EPS,
                                  ALU.mult, ALU.add).then_inc(ms_ready, 1)

            dve.memset(ms[:, :], 1.0).then_inc(own.next("ms_clear"), 1)
            own.wait("ms_clear", 1)
            square(0)
            square(1)
            square(2)
            for h in range(HH):
                if h >= 2:
                    own_rows(h)
                last_b = hF[:, h, SEQ:NT].rearrange("p (b t) -> p b t", t=DT)[:, :, DT - 1:DT]
                if h:
                    dve.wait_ge(sstate_step, 2 * h)
                dve.tensor_tensor(S_decayed[:, :, :], S0[:, :, h, :], last_b.broadcast_to([P, DB, DK]), ALU.mult).then_inc(own.next("sdecay"), 1)
                own.wait("sdecay", h + 1)
                dve.wait_ge(sgain_done, h + 1)
                for n in range(2):
                    dve.tensor_tensor(S0[:, 4 * n:4 * n + 4, h, :], S_decayed[:, 4 * n:4 * n + 4, :],
                                      psum[2 * (h % 2) + n][:, :].rearrange("p (b v) -> p b v", b=4), ALU.add).then_inc(sstate_step, 1)
            dve.wait_ge(rms_ready, 1)
            dve.reciprocal(ms[:, 0:3 * HH], ms[:, 0:3 * HH]).then_inc(own.next("ms_clear"), 1)
            own.wait("ms_clear", 2)
            dve.wait_ge(scales_ready, 5)
            for t, (t0, m) in enumerate(TILES):
                v = o_rows[0:m, t, :].rearrange("p (h n) -> p h n", h=HH)
                dve.tensor_tensor(v, v, ms[0:m, HH * t:HH * (t + 1)].unsqueeze(2).broadcast_to([m, HH, DK]), ALU.mult).then_inc(own.next("o_step"), 1)
                own.wait("o_step", 7 + t)
                dve.tensor_tensor(o_rows[0:m, t, :], o_rows[0:m, t, :], hg[0:m, t, :], ALU.mult).then_inc(o_ready, 1)
            for t, (t0, m) in enumerate(TILES):
                dve.wait_ge(hgo_turned, t + 1)
                dve.tensor_copy(hgoT[:, :, t0:t0 + m], psum[t][:, 0:HH * m].rearrange("p (h n) -> p h n", h=HH)).then_inc(hgo_copied, 1)
            dve.wait_ge(gates_ready, 2)
            for it, (g, qt) in enumerate(ITS):
                dve.wait_ge(ps_done, it + 1)
                if it == 0:
                    dve.wait_ge(state_p_stored, 16)
                else:
                    dve.wait_ge(pv_done, it)
                    dve.wait_ge(nsa_copied, it)
                diag = slice(qt * P, (qt + 1) * P)
                n_keys = (qt + 1) * P
                for h in range(HG):
                    dve.tensor_tensor(probs[:, h, :, diag], psum[h][:, :].rearrange("p (b n) -> p b n", b=2)[:, :, diag],
                                      C("causal").unsqueeze(1).broadcast_to([P, 2, P]), ALU.add).then_inc(ps_step, 1)
                dve.tensor_tensor(pc_rows, psum[4][:, 0:HG * NCP].rearrange("p (h n) -> p h n", h=HG),
                                  C("cmp_mask")[:, qt * NCP:(qt + 1) * NCP].unsqueeze(1).broadcast_to([P, HG, NCP]),
                                  ALU.add).then_inc(ps_step, 1)
                dve.wait_ge(ps_step, 5 * (it + 1))
                if qt:
                    dve.wait_ge(ps_act, PREV_ACT[it] + HG)
                dve.tensor_reduce(stat[:, 0, 0:8], probs[:, :, :, 0:n_keys].rearrange("p h b n -> p (h b) n"), AXX, ALU.max).then_inc(own.next("pw_step"), 1)
                dve.tensor_reduce(stat[:, 0, 8:12], pc_rows, AXX, ALU.max).then_inc(own.next("pw_step"), 1)
                own.wait("pw_step", 6 * it + 2)
                dve.tensor_scalar(stat[:, 0, :], stat[:, 0, :], -SCALE, None, ALU.mult).then_inc(pmax_ready, 1)
                dve.wait_ge(pexp_done, 12 * (it + 1))
                dve.reciprocal(stat[:, 1, :], stat[:, 1, :]).then_inc(own.next("pw_step"), 1)
                own.wait("pw_step", 6 * it + 3)
                dve.tensor_tensor(stat[:, 2, 0:8].rearrange("p (h b) -> p h b", b=2), stat[:, 1, 0:8].rearrange("p (h b) -> p h b", b=2),
                                  bgate[:, qt, 8:24].rearrange("p (b x) -> p x b", b=2)[:, g * HG:(g + 1) * HG, :], ALU.mult).then_inc(own.next("pw_step"), 1)
                dve.scalar_tensor_tensor(out=stat[:, 2, 8:12], in0=stat[:, 1, 8:12], scalar=C("cmp_any")[:, qt:qt + 1],
                                         in1=bgate[:, qt, g * HG:(g + 1) * HG], op0=ALU.mult, op1=ALU.mult).then_inc(own.next("pw_step"), 1)
                own.wait("pw_step", 6 * it + 5)
                for h in range(HG):
                    for br in range(2):
                        c = 2 * h + br
                        dve.tensor_scalar(probs[:, h, br, 0:n_keys], probs[:, h, br, 0:n_keys], stat[:, 2, c:c + 1], None,
                                          ALU.mult).then_inc(pp_ready, 1)
                dve.tensor_tensor(pc_rows, pc_rows, stat[:, 2, 8:12].unsqueeze(2).broadcast_to([P, HG, NCP]), ALU.mult).then_inc(pp_ready, 1)
                dve.wait_ge(pv_done, it + 1)
                rows = slice(g * DH, (g + 1) * DH)
                dve.wait_ge(pp_ready, 9 * (it + 1))
                dve.sem_inc(own.next("pw_step"), 1)
                dve.tensor_copy(nsaT[rows, :, qt * P:(qt + 1) * P], psum[7][rows, :].rearrange("p (h n) -> p h n", h=HG)).then_inc(nsa_copied, 1)
            dve.wait_ge(hgo_turned, 3)
            dve.memset(work[:, 4736:4736 + 1024], 0.0).then_inc(own.next("own_clear"), 1)
            own.wait("own_clear", 1)
            dve.wait_ge(sgate_loaded, 32)
            for s in range(2):
                if s:
                    dve.wait_ge(scores_done, 12)
                for n in range(2):
                    for g in range(G):
                        rows = slice(g * DH, (g + 1) * DH)
                        dst = work[rows, 4736 + 512 * n:4736 + 512 * n + 640].rearrange("p (b x) -> p b x", b=4)[:, :, 0:32]
                        dst = dst.rearrange("p b (t y) -> p b t y", t=DT)[:, :, :, g * HG:(g + 1) * HG]
                        for b4 in range(4):
                            c0 = SEQ + 16 * s + DT * b4
                            i = dve.tensor_copy(dst[:, b4], qT[rows, n, :, c0:c0 + DT].rearrange("p h t -> p t h"))
                        i.then_inc(q_own_ready, 1)
                dve.wait_ge(small_scores, s + 1)
                if s:
                    dve.wait_ge(st_turned, 4)
                cc = s_rows[:, 1600:1600 + NCS]
                dve.tensor_copy(cc, psum[0][:, 0:NCS]).then_inc(own.next("c_step"), 1)
                for n, c0 in enumerate((PAST, 1568)):
                    dve.tensor_tensor(s_rows[:, c0:c0 + NS], psum[0][:, 64 + NS * n:64 + NS * (n + 1)],
                                      C("new_mask")[:, NS * s:NS * (s + 1)], ALU.add).then_inc(rows_step, 1)
                own.wait("c_step", 3 * s + 1)
                dve.tensor_reduce(stat[:, 3, 2:3], cc, AXX, ALU.max).then_inc(own.next("c_step"), 1)
                own.wait("c_step", 3 * s + 2)
                dve.tensor_scalar(stat[:, 3, 0:1], stat[:, 3, 2:3], -SCALE, None, ALU.mult).then_inc(cneg_ready, 1)
                dve.wait_ge(cexp_done, s + 1)
                dve.reciprocal(stat[:, 3, 1:2], stat[:, 3, 1:2]).then_inc(own.next("c_step"), 1)
                own.wait("c_step", 3 * s + 3)
                dve.tensor_scalar(cc, cc, stat[:, 3, 1:2], None, ALU.mult).then_inc(cp_ready, 1)
                dve.wait_ge(imp_done, s + 1)
                step = own.chain("pick_step", 7 * s)
                imp, worst = pick[:, 0:14], pick[:, 14:15]
                step(dve.tensor_reduce(imp, psum[6][:, 4:4 + 56].rearrange("p (n c) -> p n c", c=4), AXX, ALU.add))
                step(dve.tensor_tensor(imp, imp, psum[6][:, 3:3 + 56].rearrange("p (n c) -> p n c", c=4)[:, :, 0], ALU.add))
                step(dve.tensor_reduce(worst, imp, AXX, ALU.min))
                step(dve.scalar_tensor_tensor(out=imp, in0=imp, scalar=worst, in1=C("block_no"), op0=ALU.is_equal, op1=ALU.mult))
                step(dve.tensor_reduce(worst, imp, AXX, ALU.max))
                step(dve.memset(drop[:, :], 0.0))
                step(dve.tensor_scalar(drop[:, 1:15], C("block_no"), worst, NEG, ALU.is_equal, ALU.mult))
                dve.tensor_scalar(cc, cc, sgate[:, s, 0:1], None, ALU.mult).then_inc(prob_ready, 1)
                dve.wait_ge(scores_done, 12 * (s + 1))
                for n in range(2):
                    dve.tensor_tensor(s_rows[:, 512 * n:512 * (n + 1)].rearrange("p (n c) -> p n c", c=SLC),
                                      psum[1 + n][:, :].rearrange("p (n c) -> p n c", c=SLC),
                                      drop[:, 8 * n:8 * (n + 1)].unsqueeze(2).broadcast_to([P, 8, SLC]), ALU.add).then_inc(rows_step, 1)
                dve.wait_ge(rows_act, s + 1)
                dve.tensor_tensor(s_rows[:, 1056:1056 + DT], psum[3][:, 0:DT], C("win_mask"), ALU.add).then_inc(rows_step, 1)
                dve.wait_ge(rows_step, 5 * (s + 1))
                step = own.chain("w_step", 5 * s)
                dve.tensor_reduce(stat[:, 3, 2:3], s_rows[:, 0:1056], AXX, ALU.max).then_inc(own.next("w_step"), 1)
                step(dve.tensor_reduce(stat[:, 3, 3:4], s_rows[:, 1056:1600], AXX, ALU.max), 2)
                dve.tensor_scalar(stat[:, 3, 4:6], stat[:, 3, 2:4], -SCALE, None, ALU.mult).then_inc(neg_ready, 1)
                dve.wait_ge(exp_done, 2 * (s + 1))
                step(dve.reciprocal(stat[:, 3, 6:8], stat[:, 3, 6:8]))
                step(dve.tensor_tensor(stat[:, 3, 6:8], stat[:, 3, 6:8], sgate[:, s, 1:3], ALU.mult))
                dve.tensor_scalar(s_rows[:, 0:1056], s_rows[:, 0:1056], stat[:, 3, 6:7], None, ALU.mult).then_inc(prob_ready, 1)
                dve.tensor_scalar(s_rows[:, 1056:1600], s_rows[:, 1056:1600], stat[:, 3, 7:8], None, ALU.mult).then_inc(prob_ready, 1)
                dve.wait_ge(prob_ready, 3 * (s + 1))
                step(dve.memset(drop[:, 16:17], 0.0))
                dve.wait_ge(spv_done, s + 1)
                for g in range(G):
                    rows = slice(g * DH, (g + 1) * DH)
                    dve.tensor_copy(nsaT[rows, :, SEQ + 16 * s:SEQ + 16 * (s + 1)].rearrange("p h t -> p t h"),
                                    psum[7][rows, 0:P].rearrange("p (t y) -> p t y", t=16)[:, :, g * HG:(g + 1) * HG]).then_inc(snsa_copied, 1)
            dve.wait_ge(snsa_copied, 4)
            dve.wait_ge(st_copied, 8)
            dve.memset(h_rows[:, 2, :], 0.0).then_inc(h_clear, 1)
            dve.wait_ge(gates_ready, 3)
            for m in range(KD):
                dve.wait_ge(ab_done, m + 1)
                if m >= 2:
                    dve.wait_ge(mix_ready, m - 1)
                for n in range(2):
                    dve.tensor_tensor(mix_t[:, m % 2, n, :], psum[2 * (m % 2) + n][:, 0:NT], gatesT[:, 8 * n + m, :], ALU.mult).then_inc(own.next("mix_step"), 1)
                own.wait("mix_step", 2 * (m + 1))
                dve.tensor_tensor(mixT[:, m, :], mix_t[:, m % 2, 0, :], mix_t[:, m % 2, 1, :], ALU.add).then_inc(mix_ready, 1)

            def norm(rows, n, g, b, ready):
                for t, (t0, m) in enumerate(TILES):
                    x = rows[0:m, t, :]
                    if n == 0:
                        own.wait("res_step", 2 * t + 2)
                    dve.tensor_reduce(ln_sum[0:m, t:t + 1], x, AXX, ALU.add).then_inc(ln_step, 1)
                    dve.wait_ge(ln_step, 9 * n + 3 * t + 1)
                    dve.tensor_scalar(ln_sum[0:m, t:t + 1], ln_sum[0:m, t:t + 1], -1.0 / D, None, ALU.mult).then_inc(ln_step, 1)
                    dve.wait_ge(ln_step, 9 * n + 3 * t + 2)
                    dve.tensor_scalar(x, x, ln_sum[0:m, t:t + 1], None, ALU.add).then_inc(ln_step, 1)
                for t, (t0, m) in enumerate(TILES):
                    dve.wait_ge(ln_sq_done, 3 * n + t + 1)
                    dve.tensor_scalar(ln_sq[0:m, t:t + 1], ln_sq[0:m, t:t + 1], 1.0 / D, LN_EPS, ALU.mult, ALU.add).then_inc(ln_var, 1)
                for t, (t0, m) in enumerate(TILES):
                    x = rows[0:m, t, :]
                    dve.wait_ge(ln_rms, 3 * n + t + 1)
                    dve.reciprocal(ln_sq[0:m, t:t + 1], ln_sq[0:m, t:t + 1]).then_inc(own.next("ln_end"), 1)
                    own.wait("ln_end", 6 * n + 2 * t + 1)
                    dve.scalar_tensor_tensor(out=x, in0=x, scalar=ln_sq[0:m, t:t + 1], in1=g[0:m, :], op0=ALU.mult, op1=ALU.mult).then_inc(own.next("ln_end"), 1)
                    own.wait("ln_end", 6 * n + 2 * t + 2)
                    dve.tensor_tensor(x, x, b[0:m, :], ALU.add).then_inc(ready, 1)

            dve.wait_ge(x_again, 64)
            for i in range(6):
                t, half = i // 2, i % 2
                m = TILES[t][1]
                x = h_rows[0:m, t, half * 512:(half + 1) * 512]
                dve.wait_ge(wo_done, i + 1)
                dve.scalar_tensor_tensor(out=x, in0=x, scalar=ALPHA, in1=psum[(4 + i) % 8][0:m, :], op0=ALU.mult, op1=ALU.add).then_inc(own.next("res_step"), 1)
            norm(h_rows, 0, ln1[:, 0, :], ln1[:, 1, :], h_ready)
            step = own.chain("route_step", 0)
            step(dve.memset(logits, 0.0))
            for t, (t0, m) in enumerate(TILES):
                dve.wait_ge(logits_done, t + 1)
                step(dve.tensor_tensor(logits[0:m, t, :], psum[4 + t][0:m, 0:NE], b_router[0:m, :], ALU.add))
                step(dve.max(top[:, t, :], logits[:, t, :]))
            dve.tensor_scalar(negtop, top[:, :, 0], -1.0, None, ALU.mult).then_inc(negtop_ready, 1)
            fourth = top[:, :, 3:4].broadcast_to([P, 3, NE])
            step(dve.tensor_tensor(above, logits, fourth, ALU.is_gt))
            step(dve.tensor_tensor(equal, logits, fourth, ALU.is_equal))
            step(dve.tensor_reduce(picked, above, AXX, ALU.add))
            for t in range(3):
                step(dve.tensor_tensor_scan(ranks[:, t, :], C("ones")[:, 0:NE], equal[:, t, :], 0.0, ALU.mult, ALU.add))
            step(dve.tensor_tensor(ranks, ranks, picked.unsqueeze(2).broadcast_to([P, 3, NE]), ALU.add))
            step(dve.scalar_tensor_tensor(out=equal, in0=ranks, scalar=4.0, in1=equal, op0=ALU.is_le, op1=ALU.mult))
            step(dve.tensor_tensor(select, above, equal, ALU.add))
            dve.tensor_tensor(select, select, C("valid").unsqueeze(2).broadcast_to([P, 3, NE]), ALU.mult).then_inc(select_ready, 1)
            dve.wait_ge(select_ready, 1)
            dve.wait_ge(ex_ready, 3)
            step(dve.tensor_tensor(equal, above, equal, ALU.add))
            step(dve.tensor_tensor(gate, gate, equal, ALU.mult))
            step(dve.tensor_reduce(picked, gate, AXX, ALU.add))
            step(dve.reciprocal(picked, picked))
            step(dve.tensor_tensor(gate, gate, picked.unsqueeze(2).broadcast_to([P, 3, NE]), ALU.mult))
            dve.wait_ge(place_done, 1)
            step(dve.scalar_tensor_tensor(out=place, in0=psum[7][:, 0:3 * NE].rearrange("p (t n) -> p t n", t=3), scalar=1.0,
                                          in1=select, op0=ALU.add, op1=ALU.mult))
            dve.tensor_scalar(place, place, -1.0, None, ALU.add).then_inc(place_ready, 1)
            step(dve.tensor_reduce(over[:, 4:5], psum[7][:, 3 * NE:4 * NE], AXX, ALU.max))
            step(dve.tensor_scalar(over[:, 0:4], C("caps"), over[:, 4:5], None, ALU.is_lt))
            step(dve.tensor_reduce(over[:, 4:5], over[:, 0:4], AXX, ALU.add))
            dve.tensor_scalar(rounds_i[:, :], over[0:1, 4:5], 1.0, None, ALU.add).then_inc(place_ready, 1)
            dve.wait_ge(y_started, 3)

            start_counts(dve, "dve")
            dve.memset(ye, 0.0).then_inc(ye_copied, 1)
            dve.memset(pgT, 0.0).then_inc(pgT_copied, 1)

            def pick_slots(e, n):
                if n is not 0:
                    dve.wait_ge(gathered, n)
                    dve.wait_ge(pg_ready, n)
                dve.tensor_tensor(pick_rows, C("slot_of").unsqueeze(1).broadcast_to([P, 3, CAP]),
                                  place[:, :, bass.ds(e, 1)].broadcast_to([P, 3, CAP]), ALU.is_equal).then_inc(pick_ready, 1)

            def activate(i):
                dve.wait_ge(gu_done, i + 1)
                dve.wait_ge(sg_ready, i + 1)
                dve.wait_ge(ug_ready, i + 1)
                dve.tensor_scalar(g_lim, psum[2][:, :], 7.0, None, ALU.min).then_inc(g_ready, 1)
                dve.wait_ge(act_ready, i + 1)
                dve.tensor_scalar(u_lim, psum[3][:, :], 7.0, -7.0, ALU.min, ALU.max).then_inc(u_ready, 1)
                dve.wait_ge(u_ready, i + 2)
                dve.wait_ge(g_ready, i + 1)
                dve.scalar_tensor_tensor(out=u_lim, in0=u_lim, scalar=1.0, in1=g_lim, op0=ALU.add, op1=ALU.mult).then_inc(ug_ready, 1)
                dve.wait_ge(ug_ready, i + 2)
                dve.wait_ge(sg_ready, i + 2)
                dve.wait_ge(act_turned, i + 1)
                dve.tensor_tensor(act_rows, u_lim, sg, ALU.mult).then_inc(act_ready, 1)

            def add_rows(i):
                for t in range(3):
                    dve.wait_ge(comb_done, i * 3 + t + 1)
                    dve.wait_ge(y_added, i * 6 + 6)
                    for half in range(2):
                        y = y_rows[:, t, half * 512:(half + 1) * 512]
                        dve.tensor_tensor(y, y, psum[6 + half][:, :], ALU.add).then_inc(y_added, 1)

            rounds = rounds_of(dve)
            pick_slots(0, 0)
            with dve.Fori(0, rounds) as r:
                with dve.Fori(0, NE - 1) as e:
                    pick_slots(e + 1, r * NE + e + 1)
                    activate(r * NE + e)
                    add_rows(r * NE + e)
                i = r * NE + (NE - 1)
                dve.wait_ge(pick_ready, i + 1)
                dve.tensor_scalar(place, place, -float(CAP), None, ALU.add).then_inc(pick_shifted, 1)
                dve.wait_ge(pick_shifted, r + 1)
                pick_slots(0, i + 1)
                activate(i)
                add_rows(i)
            add_rows(rounds * NE)
            dve.wait_ge(y_added, rounds * (6 * NE) + 12)
            dve.wait_ge(ln2_loaded, 32)
            norm(y_rows, 1, ln2[0], ln2[1], y_ready)

_INS = ["x_prompt", "x_sample", "cache_cmp_kv", "cache_slc_kv", "cache_win_kv", "state_hgrn", "page_table",
        "w_in", "pe_ck", "w_ck1", "w_ck2", "pe_cv", "w_cv1", "w_cv2", "hg_lb_logits", "hg_norm_w",
        "w_pa", "w_pb", "w_o", "ln1_g", "ln1_b", "w_router", "b_router", "w_gu", "b_gu", "w_dn", "b_dn",
        "ln2_g", "ln2_b"]
_OUTS = [("y_p", (1, SEQ, D)), ("y_s", (DB, DT, D)),
         ("cmp_p", (DEPTH, 1, SEQ, 2, G, DH)), ("cmp_s", (DEPTH, DB, DT, 2, G, DH)),
         ("slc_p", (DEPTH, 1, SEQ, 2, G, DH)), ("slc_s", (DEPTH, DB, DT, 2, G, DH)),
         ("win_p", (DEPTH, 1, SEQ, 2, G, DH)), ("win_s", (DEPTH, DB, WIN, 2, G, DH)),
         ("state_p", (DEPTH, 1, HH, DK, DK)), ("state_s", (DEPTH, DB, HH, DK, DK))]


def kernel(**inputs):
    import concourse.bacc as _bacc
    from concourse.bass_utils import run_bass_kernel_spmd as _run

    nc = _bacc.Bacc("TRN2", target_bir_lowering=False, num_devices=1)
    arrays, ins, outs = {}, {}, {}
    for name in _INS:
        a = np.ascontiguousarray(inputs[name])
        arrays[f"in_{name}"] = a
        ins[name] = nc.dram_tensor(f"in_{name}", a.shape, mybir.dt.from_np(a.dtype), kind="ExternalInput").ap()
    arrays["in_consts"] = np.ascontiguousarray(np.concatenate(list(PARTS.values()), axis=1))
    ins["consts"] = nc.dram_tensor("in_consts", (P, CONST_N), F32, kind="ExternalInput").ap()
    for name, shape in _OUTS:
        outs[name] = nc.dram_tensor(f"out_{name}", shape, F32, kind="ExternalOutput").ap()
    trunk_kernel(nc, ins, outs)
    r = _run(nc, [arrays], core_ids=[0])
    return tuple(r.results[0][f"out_{name}"] for name, _ in _OUTS)
```
